# Optimizing a Trainium2 kernel written in Bass

```python
import jax, jax.numpy as jnp
from jax import lax
import numpy as np

D_MODEL = 1024
BATCH = 1
SEQ = 256
DEPTH = 1

CHUNK = 64
PLE_DIM = 256
RW_HEADS = 8
RW_HEAD_DIM = 64
RW_WIDTH = RW_HEADS * RW_HEAD_DIM
RW_DECAY_LORA = 64
RW_ICLR_LORA = 64
RW_GATE_LORA = 128
RW_GN_EPS = 64e-5
GLA_HEADS = 4
GLA_KEY_DIM = 64
GLA_VAL_DIM = 128
GLA_QK_WIDTH = GLA_HEADS * GLA_KEY_DIM
GLA_V_WIDTH = GLA_HEADS * GLA_VAL_DIM
GLA_GATE_RANK = 16
GLA_GATE_TEMP = 16.0
MIX_WIDTH = RW_WIDTH + GLA_V_WIDTH
RW_COLS = 3 * RW_WIDTH + RW_DECAY_LORA + RW_ICLR_LORA + RW_GATE_LORA
GLA_COLS = 2 * GLA_QK_WIDTH + 2 * GLA_V_WIDTH + GLA_GATE_RANK
IN_COLS = RW_COLS + GLA_COLS
N_EXPERTS = 32
TOP_K = 4
D_FF = 1024
SWIGLU_ALPHA = 1.702
SWIGLU_LIMIT = 7.0
EXPERT_BLOCK = 256
NORM_EPS = 1e-6

kernel_name = "hybrid_rwkv7_gla_moe_ple_block"

def rmsnorm(x, g):
    xf = x.astype(jnp.float32)
    y = xf * lax.rsqrt(jnp.mean(xf * xf, axis=-1, keepdims=True) + NORM_EPS)
    return (y * g.astype(jnp.float32)).astype(x.dtype)

def token_shift(h, mu):
    prev = jnp.pad(h, ((0, 0), (1, 0), (0, 0)))[:, :-1]
    return h + (prev - h) * mu

def rwkv7_mix(h, w0, w2, a0, a2, g2, k_k, k_a, r_k, gn_w, gn_b):
    B, S, _ = h.shape
    H, D = RW_HEADS, RW_HEAD_DIM
    f32 = jnp.float32
    o0 = 0
    r = h[..., o0:o0 + RW_WIDTH]; o0 += RW_WIDTH
    k = h[..., o0:o0 + RW_WIDTH]; o0 += RW_WIDTH
    v = h[..., o0:o0 + RW_WIDTH]; o0 += RW_WIDTH
    dw = h[..., o0:o0 + RW_DECAY_LORA]; o0 += RW_DECAY_LORA
    da = h[..., o0:o0 + RW_ICLR_LORA]; o0 += RW_ICLR_LORA
    dg = h[..., o0:o0 + RW_GATE_LORA]

    w_log = -jax.nn.softplus(-(w0 + jnp.tanh(dw) @ w2)) - 0.5
    decay = jnp.exp(-jnp.exp(w_log.astype(f32)))
    iclr = jax.nn.sigmoid((a0 + da @ a2).astype(f32))
    gate = jax.nn.sigmoid(dg) @ g2

    kk = (k * k_k).astype(f32).reshape(B, S, H, D)
    kk = kk / jnp.maximum(jnp.sqrt(jnp.sum(kk * kk, -1, keepdims=True)), 1e-12)
    k = k.astype(f32) * (1.0 + (iclr - 1.0) * k_a.astype(f32))

    def heads(t):
        return t.astype(f32).reshape(B, S, H, D)

    r4, k4, v4, w4, a4 = heads(r), heads(k), heads(v), heads(decay), heads(iclr)

    def tm(t):
        return jnp.transpose(t, (1, 0, 2, 3))

    def step(state, inp):
        r_t, w_t, k_t, v_t, kk_t, a_t = inp
        sa = jnp.einsum('bhvk,bhk->bhv', state, -kk_t)
        state = (state * w_t[:, :, None, :]
                 + sa[..., None] * (kk_t * a_t)[:, :, None, :]
                 + v_t[..., None] * k_t[:, :, None, :])
        return state, jnp.einsum('bhvk,bhk->bhv', state, r_t)

    s0 = jnp.zeros((B, H, D, D), f32)
    _, o = lax.scan(step, s0, (tm(r4), tm(w4), tm(k4), tm(v4), tm(kk), tm(a4)))
    o = jnp.transpose(o, (1, 0, 2, 3))

    mu = jnp.mean(o, -1, keepdims=True)
    var = jnp.mean(jnp.square(o - mu), -1, keepdims=True)
    o = ((o - mu) * lax.rsqrt(var + RW_GN_EPS)).reshape(B, S, RW_WIDTH)
    o = o * gn_w.astype(f32) + gn_b.astype(f32)
    bonus = jnp.sum(r4 * k4 * r_k.astype(f32), -1, keepdims=True) * v4
    o = (o + bonus.reshape(B, S, RW_WIDTH)) * gate.astype(f32)
    return o.astype(h.dtype)

def gla_mix(h, gk2, gk_b, norm_g):
    B, S, _ = h.shape
    H, DK, DV = GLA_HEADS, GLA_KEY_DIM, GLA_VAL_DIM
    f32 = jnp.float32
    o0 = 0
    q = h[..., o0:o0 + GLA_QK_WIDTH]; o0 += GLA_QK_WIDTH
    k = h[..., o0:o0 + GLA_QK_WIDTH]; o0 += GLA_QK_WIDTH
    v = h[..., o0:o0 + GLA_V_WIDTH]; o0 += GLA_V_WIDTH
    g = h[..., o0:o0 + GLA_V_WIDTH]; o0 += GLA_V_WIDTH
    dgk = h[..., o0:o0 + GLA_GATE_RANK]

    log_a = jax.nn.log_sigmoid((dgk @ gk2 + gk_b).astype(f32)) / GLA_GATE_TEMP
    q = q.astype(f32) * (DK ** -0.5)
    NC = S // CHUNK

    def chunks(t, d):
        return t.astype(f32).reshape(B, NC, CHUNK, H, d).transpose(1, 0, 3, 2, 4)

    causal = jnp.tril(jnp.ones((CHUNK, CHUNK), bool))[:, :, None]

    def step(state, inp):
        qc, kc, vc, lac = inp
        b = jnp.cumsum(lac, axis=2)
        o_inter = jnp.einsum('bhcd,bhdv->bhcv', qc * jnp.exp(b), state)
        diff = b[:, :, :, None, :] - b[:, :, None, :, :]
        dec = jnp.exp(jnp.where(causal, diff, -jnp.inf))
        att = jnp.einsum('bhid,bhjd,bhijd->bhij', qc, kc, dec)
        o = o_inter + jnp.einsum('bhij,bhjv->bhiv', att, vc)
        b_last = b[:, :, -1:, :]
        state = (jnp.exp(b_last[:, :, 0, :])[..., None] * state
                 + jnp.einsum('bhjd,bhjv->bhdv', kc * jnp.exp(b_last - b), vc))
        return state, o

    s0 = jnp.zeros((B, H, DK, DV), f32)
    _, o = lax.scan(step, s0, (chunks(q, DK), chunks(k, DK), chunks(v, DV), chunks(log_a, DK)))
    o = o.transpose(1, 0, 3, 2, 4).reshape(B, S, H, DV)
    o = o * lax.rsqrt(jnp.mean(o * o, -1, keepdims=True) + NORM_EPS)
    o = o.reshape(B, S, GLA_V_WIDTH) * norm_g.astype(f32) * jax.nn.silu(g.astype(f32))
    return o.astype(h.dtype)

def moe(u, w_router, b_router, w1, b1, w2, b2):
    B, S, D = u.shape
    N = B * S
    A = N * TOP_K
    NB = (A + N_EXPERTS * (EXPERT_BLOCK - 1) + EXPERT_BLOCK - 1) // EXPERT_BLOCK
    xf = u.reshape(N, D)
    logits = (xf @ w_router + b_router).astype(jnp.float32)
    top_v, top_i = lax.top_k(logits, TOP_K)
    gates = jax.nn.softmax(top_v, axis=-1).astype(xf.dtype)

    flat_e = top_i.reshape(-1).astype(jnp.int32)
    flat_tok = jnp.arange(A, dtype=jnp.int32) // TOP_K
    flat_w = gates.reshape(-1)
    order = jnp.argsort(flat_e, stable=True)
    e_s, tok_s, w_s = flat_e[order], flat_tok[order], flat_w[order]

    counts = jax.ops.segment_sum(jnp.ones((A,), jnp.int32), flat_e, num_segments=N_EXPERTS)
    start = jnp.cumsum(counts) - counts
    pcounts = ((counts + EXPERT_BLOCK - 1) // EXPERT_BLOCK) * EXPERT_BLOCK
    pend = jnp.cumsum(pcounts)
    pstart = pend - pcounts
    dest = pstart[e_s] + (jnp.arange(A, dtype=jnp.int32) - start[e_s])

    tok_buf = jnp.zeros((NB * EXPERT_BLOCK,), jnp.int32).at[dest].set(tok_s)
    w_buf = jnp.zeros((NB * EXPERT_BLOCK,), xf.dtype).at[dest].set(w_s)
    block_rows = jnp.arange(NB, dtype=jnp.int32) * EXPERT_BLOCK
    block_e = jnp.clip(jnp.searchsorted(pend, block_rows, side='right'), 0, N_EXPERTS - 1)

    def expert_block(args):
        tok_b, w_b, e = args
        xb = xf[tok_b]
        hgl = xb @ w1[e] + b1[e]
        x_glu = jnp.minimum(hgl[:, :D_FF], SWIGLU_LIMIT)
        x_lin = jnp.clip(hgl[:, D_FF:], -SWIGLU_LIMIT, SWIGLU_LIMIT)
        act = (x_lin + 1.0) * (x_glu * jax.nn.sigmoid(SWIGLU_ALPHA * x_glu))
        return (act @ w2[e] + b2[e]) * w_b[:, None]

    ys = lax.map(expert_block, (tok_buf.reshape(NB, EXPERT_BLOCK),
                                w_buf.reshape(NB, EXPERT_BLOCK), block_e))
    out = jnp.zeros_like(xf).at[tok_buf].add(ys.reshape(-1, D))
    return out.reshape(B, S, D)

def setup_inputs(seed: int = 0) -> dict:
    key = jax.random.key(seed)
    ks = jax.random.split(key, 40)
    f32 = jnp.float32

    def nrm(k, shape, scale):
        return jax.random.normal(k, shape, f32) * scale

    def gain(k, shape):
        return 1.0 + 0.05 * jax.random.normal(k, shape, f32)

    L, D, E, F = DEPTH, D_MODEL, N_EXPERTS, D_FF
    return {
        "x": nrm(ks[0], (BATCH, SEQ, D), 1.0),
        "p": nrm(ks[1], (L, BATCH, SEQ, PLE_DIM), 1.0),
        "norm_mix": gain(ks[2], (L, D)),
        "w_in": nrm(ks[3], (L, D, IN_COLS), D ** -0.5),
        "shift_mu": jax.random.uniform(ks[4], (L, RW_COLS), f32),
        "rw_w0": jax.random.uniform(ks[5], (L, RW_WIDTH), f32, -6.0, -1.0),
        "rw_w2": nrm(ks[6], (L, RW_DECAY_LORA, RW_WIDTH), 0.1),
        "rw_a0": nrm(ks[7], (L, RW_WIDTH), 0.5),
        "rw_a2": nrm(ks[8], (L, RW_ICLR_LORA, RW_WIDTH), 0.5 * RW_ICLR_LORA ** -0.5),
        "rw_g2": nrm(ks[9], (L, RW_GATE_LORA, RW_WIDTH), RW_GATE_LORA ** -0.5),
        "rw_kk": 0.85 + 0.05 * jax.random.normal(ks[10], (L, RW_WIDTH), f32),
        "rw_ka": gain(ks[11], (L, RW_WIDTH)),
        "rw_rk": nrm(ks[12], (L, RW_HEADS, RW_HEAD_DIM), 0.1),
        "rw_gn_w": gain(ks[13], (L, RW_WIDTH)),
        "rw_gn_b": nrm(ks[14], (L, RW_WIDTH), 0.01),
        "gla_gk2": nrm(ks[15], (L, GLA_GATE_RANK, GLA_QK_WIDTH), GLA_GATE_RANK ** -0.5),
        "gla_gk_b": nrm(ks[16], (L, GLA_QK_WIDTH), 0.1),
        "gla_norm": gain(ks[17], (L, GLA_V_WIDTH)),
        "w_out": nrm(ks[18], (L, MIX_WIDTH, D), MIX_WIDTH ** -0.5),
        "norm_ffn": gain(ks[19], (L, D)),
        "w_router": nrm(ks[20], (L, D, E), D ** -0.5),
        "b_router": nrm(ks[21], (L, E), 0.01),
        "w1": nrm(ks[22], (L, E, D, 2 * F), D ** -0.5),
        "b1": nrm(ks[23], (L, E, 2 * F), 0.01),
        "w2": nrm(ks[24], (L, E, F, D), F ** -0.5),
        "b2": nrm(ks[25], (L, E, D), 0.01),
        "norm_ple": gain(ks[26], (L, D)),
        "w_ple_gate": nrm(ks[27], (L, D, D), D ** -0.5),
        "w_ple": nrm(ks[28], (L, PLE_DIM, D), PLE_DIM ** -0.5),
        "norm_final": gain(ks[29], (D,)),
    }

def reference(x, p, norm_mix, w_in, shift_mu, rw_w0, rw_w2, rw_a0, rw_a2, rw_g2,
              rw_kk, rw_ka, rw_rk, rw_gn_w, rw_gn_b, gla_gk2, gla_gk_b, gla_norm,
              w_out, norm_ffn, w_router, b_router, w1, b1, w2, b2,
              norm_ple, w_ple_gate, w_ple, norm_final):
    h = x
    for i in range(DEPTH):
        u = rmsnorm(h, norm_mix[i])
        proj = u @ w_in[i]
        rw_in = token_shift(proj[..., :RW_COLS], shift_mu[i])
        y_rw = rwkv7_mix(rw_in, rw_w0[i], rw_w2[i], rw_a0[i], rw_a2[i], rw_g2[i],
                         rw_kk[i], rw_ka[i], rw_rk[i], rw_gn_w[i], rw_gn_b[i])
        y_gla = gla_mix(proj[..., RW_COLS:], gla_gk2[i], gla_gk_b[i], gla_norm[i])
        h = h + jnp.concatenate([y_rw, y_gla], axis=-1) @ w_out[i]
        u = rmsnorm(h, norm_ffn[i])
        h = h + moe(u, w_router[i], b_router[i], w1[i], b1[i], w2[i], b2[i])
        u = rmsnorm(h, norm_ple[i])
        h = h + jax.nn.sigmoid(u @ w_ple_gate[i]) * (p[i] @ w_ple[i])
    return rmsnorm(h, norm_final)


_drawn_inputs = setup_inputs


def setup_inputs(seed=0):
    import zlib

    import numpy as np

    out = dict(_drawn_inputs(seed))
    spreads = {}
    factors = {'rw_gn_b': 6.172, 'b1': 8.0, 'b2': 8.0, 'norm_ple': 7.226, 'b_router': 2.68}
    for name, (base, spread) in spreads.items():
        noise = np.random.default_rng([zlib.crc32(name.encode()), seed]).standard_normal(out[name].shape)
        drawn = base * np.exp(spread * noise) if base else spread * noise
        out[name] = __import__('jax').numpy.asarray(drawn.astype(out[name].dtype))
    for name, factor in factors.items():
        out[name] = (out[name] * factor).astype(out[name].dtype)
    return out
```

```python
from contextlib import ExitStack
from math import exp

import concourse.bass as bass
from concourse import mybir

F32 = mybir.dt.float32
I32 = mybir.dt.int32
ALU = mybir.AluOpType
ACT = mybir.ActivationFunctionType
AX = mybir.AxisListType

P = 128
T = 256
TT = T // P
D = 1024
KC = D // P
L = 64
NCH = T // L
RW = 512
HP = 4
NH = 8
RWC = 3 * RW + 256
GH = 4
GQ = 256
GV_W = 512
NE = 32
FF = 1024
SLOTS = 64
NBMAX = T // SLOTS
SLOT_F = 2048
NSLOT = 12
BANK = 512
NEG = -1.0e30
EPS = 1e-6
GN_EPS = 64e-5
DECAY = exp(-0.5)
TEMP = 16.0
LEVELS = [2, 4, 8, 16, 32]

VROWS = [("norm_mix", 8), ("norm_ffn", 8), ("norm_ple", 8), ("shift_mu", 14), ("rw_w0", 4), ("rw_a0", 4),
         ("rw_kk", 4), ("rw_ka", 4), ("rw_rk", 4), ("gla_gk_b", 2)]
VAT = {}
_n = 0
for _name, _k in VROWS:
    VAT[_name] = _n
    _n += _k
NV = _n


def hybrid_block(nc, x, p, norm_mix, w_in, shift_mu, rw_w0, rw_w2, rw_a0, rw_a2, rw_g2, rw_kk, rw_ka, rw_rk,
                 rw_gn_w, rw_gn_b, gla_gk2, gla_gk_b, gla_norm, w_out, norm_ffn, w_router, b_router,
                 w1, b1, w2, b2, norm_ple, w_ple_gate, w_ple, norm_final, out):
    vec_src = {
        "norm_mix": norm_mix.rearrange("a (n q) -> (a n) q", q=P), "norm_ffn": norm_ffn.rearrange("a (n q) -> (a n) q", q=P),
        "norm_ple": norm_ple.rearrange("a (n q) -> (a n) q", q=P), "shift_mu": shift_mu.rearrange("a (n q) -> (a n) q", q=P),
        "rw_w0": rw_w0.rearrange("a (n q) -> (a n) q", q=P), "rw_a0": rw_a0.rearrange("a (n q) -> (a n) q", q=P),
        "rw_kk": rw_kk.rearrange("a (n q) -> (a n) q", q=P), "rw_ka": rw_ka.rearrange("a (n q) -> (a n) q", q=P),
        "rw_rk": rw_rk.rearrange("a (n h) q -> (a n) (h q)", h=2), "gla_gk_b": gla_gk_b.rearrange("a (n q) -> (a n) q", q=P),
    }
    with ExitStack() as ctx:
        def sem(name):
            return ctx.enter_context(nc.semaphore(name))

        RING = ctx.enter_context(nc.sbuf_tensor("ring", [P, NSLOT * SLOT_F], F32))
        PS = ctx.enter_context(nc.psum_tensor("ps", [P, 8 * BANK], F32))

        def sb(name, n, dt=F32):
            return ctx.enter_context(nc.sbuf_tensor(name, [P, n], dt))

        def slot(i, n=1):
            return RING[:, i * SLOT_F:(i + n) * SLOT_F]

        def bank(b, n=1):
            return PS[:, b * BANK:(b + n) * BANK]

        XB = sb("xb", 2048)
        UT = sb("ut", 2048)
        T34 = sb("t34", 2048)
        KRR = sb("krr", 2048)
        AR = sb("ar", 2048)
        BK = sb("bk", 2048)
        AY = sb("ay", 2048)
        BKV = sb("bkv", 3072)
        GVG = sb("gvg", 2048)
        GQK = sb("gqk", 1024)
        LB = sb("lb", 768)
        VEC = sb("vec", P)
        VC = sb("vc", 64)
        OMU = sb("omu", 16)
        OMKA = sb("omka", 4)
        LW = sb("lw", RW)
        G2 = sb("g2", RW)
        GK2 = sb("gk2", GQ)
        DGW = sb("dgw", KC * 16)
        WR = sb("wr", KC * NE)
        BR = sb("br", NE)
        MK = sb("mk", 512)
        SL = sb("sl", P)
        SU = sb("su", P)
        D1L = sb("d1l", P)
        D1U = sb("d1u", P)
        DL = sb("dl", 5 * P)
        BD = sb("bd", P)
        BDG = sb("bdg", 256)
        ID = sb("id", P)
        ONES = sb("ones", P)
        RM = sb("rm", T)
        IOTA = sb("iota", P)
        PLC = sb("plc", 16)
        EM = sb("em", 24)
        BON = sb("bon", 16)
        SM = sb("sm", 128)
        SM2 = sb("sm2", 64)
        POSB = sb("posb", NBMAX * TT * (NE + 1))
        GATES = sb("gates", TT * (NE + 1))
        RT = sb("rt", 8 * 72)
        GT = sb("gt", T)
        OH = sb("oh", TT * SLOTS)
        OHG = sb("ohg", TT * P)
        OHGT = sb("ohgt", T)
        CNT = sb("cnt", NE)
        CMAX = sb("cmax", 1)
        CNTI = sb("cnti", 1, I32)

        T1, T2 = XB[:, 0:1024], XB[:, 1024:2048]
        T3, T4 = T34[:, 0:1024], T34[:, 1024:2048]
        KR, RR = KRR[:, 0:1024], KRR[:, 1024:2048]
        BF, KF = BK[:, 0:1024], BK[:, 1024:2048]
        Bt, Kt, Vt = BKV[:, 0:1024], BKV[:, 1024:2048], BKV[:, 2048:3072]
        GV, GG = GVG[:, 0:1024], GVG[:, 1024:2048]
        L1, L2, DGK = LB[:, 0:256], LB[:, 256:512], LB[:, 512:768]
        XB3 = XB[:, :].rearrange("p (t d) -> p t d", t=TT)
        UT3 = UT[:, :].rearrange("p (k t) -> p k t", k=KC)
        AR5 = AR[:, :].rearrange("p (h t w c) -> p h t w c", h=HP, t=TT, w=2)
        AY4 = AY[:, :].rearrange("p (t h w) -> p t h w", t=TT, h=NH)
        WR3 = WR[:, :].rearrange("p (k e) -> p k e", k=KC)

        def hp3(a):
            return a.rearrange("p (h t) -> p h t", h=HP)

        MT = slot(0, 4).rearrange("p (m w) -> p m w", m=16)
        TAB = slot(4).rearrange("p (m w) -> p m w", m=16)
        X_ = slot(5).rearrange("p (m w) -> p m w", m=16)
        XT_ = slot(6).rearrange("p (m w) -> p m w", m=16)
        Y_ = slot(7).rearrange("p (m w) -> p m w", m=16)
        QE, KE, QB, KL = (slot(8)[:, 512 * i:512 * (i + 1)].rearrange("p (h t) -> p h t", h=2) for i in range(4))
        ATT = slot(9)[:, 0:1024].rearrange("p (t h w) -> p t h w", t=TT, h=GH)
        KLT = slot(9)[:, 1024:1536].rearrange("p (t h w) -> p t h w", t=TT, h=2)
        SG = slot(9)[:, 1536:2048]
        GLT = [slot(7)[:, 512 * i:512 * (i + 1)] for i in range(4)]
        WU = slot(10).rearrange("p (w t h d) -> p w t h d", w=2, t=TT, h=NH)
        WM, U0 = (slot(10)[:, 1024 * i:1024 * (i + 1)].rearrange("p (t c) -> p t c", t=TT) for i in range(2))
        REFF = slot(11)[:, 0:1024].rearrange("p (t h w) -> p t h w", t=TT, h=HP)
        GTS = slot(11)[:, 1024:2048].rearrange("p (c h w) -> p c h w", c=2, h=HP)
        HS_ = T34[:, 0:1536].rearrange("p (c w) -> p c w", c=3)
        SRW = BK[:, 0:1536].rearrange("p (c h w) -> p c h w", c=3, h=HP)
        ROWS = UT[:, 0:1536].rearrange("p (r w) -> p r w", r=3)
        YT = AR[:, :].rearrange("p (t d) -> p t d", t=TT)
        U2 = BK[:, :].rearrange("p (t d) -> p t d", t=TT)
        HS = T34[:, 0:1024]
        TP = T34[:, 1024:2048].rearrange("p (c w) -> p c w", c=KC)
        XG = GQK[:, 0:512].rearrange("p (k s) -> p k s", k=KC)
        GLU, LIN, SIG, ACTT = (AY[:, 512 * i:512 * (i + 1)].rearrange("p (k s) -> p k s", k=KC) for i in range(4))
        YS = GVG[:, 0:512]
        B1T = GVG[:, 512:512 + NE * 16].rearrange("p (e c g) -> p e c g", e=NE, g=2)
        GTMP = KRR[:, 1024:2048]
        GSIG = KRR[:, 0:1024]
        B1R, B2R, NF = BKV[:, 0:2048], BKV[:, 2048:3072], BKV[:, 0:1024]
        OH3 = OH[:, :].rearrange("p (t s) -> p t s", t=TT)
        OHG3 = OHG[:, :].rearrange("p (t s) -> p t s", t=TT)
        POS4 = POSB[:, :].rearrange("p (b t e) -> p b t e", b=NBMAX, t=TT)
        GAT3 = GATES[:, :].rearrange("p (t e) -> p t e", t=TT)
        RT8 = [RT[:, 72 * i:72 * (i + 1)].rearrange("p (t e) -> p t e", t=TT) for i in range(8)]
        PLG = slot(0, 4).rearrange("p (k n) -> p k n", k=KC)
        PLW = slot(4).rearrange("p (k n) -> p k n", k=2)
        PX = slot(5)[:, 0:512].rearrange("p (t n) -> p t n", t=TT)
        PT = slot(5)[:, 512:1024].rearrange("p (k t) -> p k t", k=2)
        ZG = AR[:, :]

        def col(name, i, n=1):
            return VC[:, VAT[name] + i:VAT[name] + i + n]

        x_in, vec_in, small_in, rows_in, wout_in, brow_in, out_done = (
            sem(s) for s in ("x_in", "vec_in", "small_in", "rows_in", "wout_in", "brow_in", "out_done"))
        win = [sem(f"win{i}") for i in range(8)]
        landed = [sem(f"landed{i}") for i in range(NSLOT)]
        ple_in = sem("ple_in")
        masks, id_ok = sem("masks"), sem("id_ok")
        vec_t, vc_ok = sem("vec_t"), sem("vc_ok")
        rstd_sq, scaled = sem("rstd_sq"), sem("scaled")
        xt_ps, ut_v, ut_a = sem("xt_ps"), sem("ut_v"), sem("ut_a")
        tile_ps, tile_a, tile_v, tile_g = sem("tile_ps"), sem("tile_a"), sem("tile_v"), sem("tile_g")
        lora_act, z_ps, a_ps, sz_ok, iclr_ok = sem("lora_act"), sem("z_ps"), sem("a_ps"), sem("sz_ok"), sem("iclr_ok")
        sq_ok, ss_ps, ss_max, nrm_ok = sem("sq_ok"), sem("ss_ps"), sem("ss_max"), sem("nrm_ok")
        gv_ps, gg_ps, gk_ps, gvg_ok = sem("gv_ps"), sem("gg_ps"), sem("gk_ps"), sem("gvg_ok")
        cs_ok, exp_ok, exp_used = sem("cs_ok"), sem("exp_ok"), sem("exp_used")
        kf_ok, a_ok, r_ok, rkk_ok = sem("kf_ok"), sem("a_ok"), sem("r_ok"), sem("rkk_ok")
        tok_ps, tok_a, tok_v, bon_ps, bon_ok = sem("tok_ps"), sem("tok_a"), sem("tok_v"), sem("bon_ps"), sem("bon_ok")
        mat_ps, mat_ok, x1_ok, x1t_ok = sem("mat_ps"), sem("mat_ok"), sem("x1_ok"), sem("x1t_ok")
        y_ps, y_ok, xx_ps, xx_ok = sem("y_ps"), sem("y_ok"), sem("xx_ps"), sem("xx_ok")
        mv_ps, mv_ok, wu_ps, wu_ok = sem("mv_ps"), sem("mv_ok"), sem("wu_ps"), sem("wu_ok")
        reff_ps, reff_ok, h_ps, gt_ps, st_ok, st_ps = (
            sem("reff_ps"), sem("reff_ok"), sem("h_ps"), sem("gt_ps"), sem("st_ok"), sem("st_ps"))
        o_ps, gate_ps, osq_v, osq_a, ovar, orstd, y_rw = (
            sem("o_ps"), sem("gate_ps"), sem("osq_v"), sem("osq_a"), sem("ovar"), sem("orstd"), sem("y_rw"))
        gx_ok, gln_ok, gla_la, gb_ok, gdiff, gexp, gla_el = (
            sem("gx_ok"), sem("gln_ok"), sem("gla_la"), sem("gb_ok"), sem("gdiff"), sem("gexp"), sem("gla_el"))
        klt_ps, klt_ok, att_ps, att_ok, sg_ps, sg_ok, go_ps, gsig, ggn = (
            sem("klt_ps"), sem("klt_ok"), sem("att_ps"), sem("att_ok"), sem("sg_ps"), sem("sg_ok"), sem("go_ps"), sem("gsig"), sem("ggn"))
        y_gla, bv_ok = sem("y_gla"), sem("bv_ok")
        wout_ps, wout_used, lg_ps, lg_max, lg_exp, sel_ok, pos_ps, cnt_ok, gt_ok, gtt_ps, gates_ok = (
            sem("wout_ps"), sem("wout_used"), sem("lg_ps"), sem("lg_max"), sem("lg_exp"), sem("sel_ok"), sem("pos_ps"), sem("cnt_ok"),
            sem("gt_ok"), sem("gtt_ps"), sem("gates_ok"))
        b1_ps, b1_ok = sem("b1_ps"), sem("b1_ok")
        oh_ok, ohg_ok, gathered, xg_ok = sem("oh_ok"), sem("ohg_ok"), sem("gathered"), sem("xg_ok")
        h0_ps, w1_used, hs0, hs1 = sem("h0_ps"), sem("w1_used"), sem("hs0"), sem("hs1")
        scattered, ohgt_ps, ohgt_ok, t_ps, t_ok = sem("scattered"), sem("ohgt_ps"), sem("ohgt_ok"), sem("t_ps"), sem("t_ok")
        glu_ok, sig_ok, act_ok, w2_used, ys_ok = sem("glu_ok"), sem("sig_ok"), sem("act_ok"), sem("w2_used"), sem("ys_ok")
        acc_done, pt_ps, pt_ok, pg_ps, pw_ps, psig = (
            sem("acc_done"), sem("pt_ps"), sem("pt_ok"), sem("pg_ps"), sem("pw_ps"), sem("psig"))
        fin = sem("fin")
        vch, ach, gch = sem("vch"), sem("ach"), sem("gch")
        xs_ok, u2_ok, go_used, lin_ok, gl_ok, gk_read = (
            sem("xs_ok"), sem("u2_ok"), sem("go_used"), sem("lin_ok"), sem("gl_ok"), sem("gk_read"))

        def linker(eng, chain):
            count = {}

            def signal(ins, s=None):
                s = s or chain
                count[id(s)] = count.get(id(s), 0) + 1
                ins.then_inc(s, 1)
                return s

            def settle(s=None):
                s = s or chain
                eng.wait_ge(s, count[id(s)])

            def link(ins, s=None):
                settle(signal(ins, s))

            return signal, settle, link

        w1_v = w1.rearrange("a e (k q) n -> a e q k n", q=P)
        w2_v = w2.rearrange("a e (k q) n -> a e q k n", q=P)

        def body_counts(nb):
            return nb, nb - 1

        block = ctx.enter_context(nc.Block())

        @block.sync
        def _(sp):
            sp.dma_start(XB3, x.rearrange("a (t q) d -> q (a t) d", q=P)).then_inc(x_in, 16)
            for name, k in VROWS:
                sp.dma_start(VEC[VAT[name]:VAT[name] + k, :], vec_src[name]).then_inc(vec_in, 16)

            def load_cols(i, s, n, c0, w):
                dst = RING[:, s * SLOT_F:s * SLOT_F + KC * w].rearrange("p (k n) -> p k n", k=KC)
                sp.dma_start(dst, w_in[0, :, c0:c0 + w].rearrange("(k q) n -> q k n", q=P)).then_inc(win[i], 16)

            load_cols(0, 0, 1, 3 * RW, 256)
            sp.dma_start(LW[0:64, :], rw_w2[0]).then_inc(small_in, 16)
            sp.dma_start(LW[64:128, :], rw_a2[0]).then_inc(small_in, 16)
            sp.dma_start(G2[:, :], rw_g2[0]).then_inc(small_in, 16)
            sp.dma_start(GK2[0:16, :], gla_gk2[0]).then_inc(small_in, 16)
            sp.dma_start(DGW[:, :].rearrange("p (k n) -> p k n", k=KC),
                         w_in[0, :, RWC + 2 * GQ + 2 * GV_W:].rearrange("(k q) n -> q k n", q=P)).then_inc(small_in, 16)
            sp.dma_start(WR3, w_router[0].rearrange("(k q) e -> q k e", q=P)).then_inc(small_in, 16)
            sp.dma_start(BR[0:1, :], b_router).then_inc(small_in, 16)
            load_cols(1, 1, 2, RW, 512)
            load_cols(2, 3, 2, 0, 512)
            load_cols(3, 5, 2, 2 * RW, 512)
            load_cols(4, 7, 2, RWC, 512)
            load_cols(5, 9, 2, RWC + 2 * GQ, 512)
            load_cols(6, 11, 1, RWC + 2 * GQ + GV_W, 256)
            sp.wait_ge(tile_ps, 2)
            load_cols(7, 0, 1, RWC + 2 * GQ + GV_W + 256, 256)
            sp.wait_ge(gg_ps, 1)
            for r, src in enumerate((rw_gn_w, rw_gn_b, gla_norm)):
                sp.dma_start(ROWS[:, r, :], src[0].partition_broadcast(P)).then_inc(rows_in, 16)
            sp.wait_ge(rkk_ok, 1)
            sp.wait_ge(bon_ps, 1)
            sp.wait_ge(r_ok, 1)
            sp.dma_start(XB3, x.rearrange("a (t q) d -> q (a t) d", q=P)).then_inc(x_in, 16)
            sp.wait_ge(wu_ok, 4)
            sp.dma_start(slot(4, 4).rearrange("p (k n) -> p k n", k=KC),
                         w_out[0].rearrange("(k q) n -> q k n", q=P)).then_inc(wout_in, 16)
            sp.wait_ge(o_ps, 1)
            sp.wait_ge(bv_ok, 1)
            sp.dma_start(B1R[0:NE, :], b1[0]).then_inc(brow_in, 16)
            sp.dma_start(B2R[0:NE, :], b2[0]).then_inc(brow_in, 16)

            def load_w1(e, k):
                sp.dma_start(slot(k), w1_v[0, e, :, k, :]).then_inc(landed[k], 16)

            def load_w2(e, j):
                sp.dma_start(slot(8 + j).rearrange("p (k n) -> p k n", k=2), w2_v[0, e, :, 2 * j:2 * j + 2, :]
                             ).then_inc(landed[8 + j], 16)

            for k in range(4):
                load_w1(0, k)
            sp.wait_ge(y_gla, 1)
            sp.wait_ge(wout_used, 1)
            for k in range(4, 8):
                load_w1(0, k)
            for j in range(4):
                load_w2(0, j)
            sp.wait_ge(b1_ok, 1)
            sp.dma_start(NF, norm_final.partition_broadcast(P)).then_inc(brow_in, 16)

            def stream(nb):
                last = nb - 1
                with sp.Fori(1, NE) as e:
                    for k in range(KC):
                        sp.wait_ge(w1_used, e * (nb * KC) + (k + 1 - KC))
                        sp.dma_start(slot(k), w1_v[0, e, :, k, :]
                                     ).then_inc(landed[k], 16)
                    for j in range(4):
                        sp.wait_ge(w2_used, e * (nb * 4) + (j + 1 - 4))
                        sp.dma_start(slot(8 + j).rearrange("p (k n) -> p k n", k=2),
                                     w2_v[0, e, :, 2 * j:2 * j + 2, :]
                                     ).then_inc(landed[8 + j], 16)
                sp.wait_ge(w1_used, NE * nb * KC)

            sp.wait_ge(cnt_ok, 1)
            most = sp.value_load(CNTI[0:1, 0:1], min_val=0, max_val=T)
            with sp.If(most > SLOTS):
                stream(NBMAX)
            with sp.Else():
                stream(1)
            sp.dma_start(PX, p.rearrange("a b (t q) n -> q (a b t) n", q=P)).then_inc(ple_in, 16)
            sp.dma_start(PLW, w_ple[0].rearrange("(k q) n -> q k n", q=P)).then_inc(ple_in, 16)
            sp.dma_start(PLG, w_ple_gate[0].rearrange("(k q) n -> q k n", q=P)).then_inc(ple_in, 16)
            sp.wait_ge(fin, 1)
            sp.dma_start(out.rearrange("a (t q) d -> q (a t) d", q=P), U2).then_inc(out_done, 16)
            sp.wait_ge(out_done, 16)

        @block.gpsimd
        def _(pool):
            signal, settle, link = linker(pool, gch)
            ones = T34[:, 0:P]
            bds = [T34[:, P * (i + 1):P * (i + 2)] for i in range(7)]

            def block_diagonal(dst, s, width):
                v = dst.rearrange("p (b c) -> p b c", c=width)
                nb = v.shape[1]
                link(pool.memset(dst, 1.0))
                link(pool.affine_select(out=v, in_=v, compare_op=ALU.is_ge, fill=0.0, base=0,
                                        pattern=[[-s, nb], [0, width]], channel_multiplier=1))
                link(pool.affine_select(out=v, in_=v, compare_op=ALU.is_ge, fill=0.0, base=s - 1,
                                        pattern=[[s, nb], [0, width]], channel_multiplier=-1))

            link(pool.memset(ones, 1.0))
            block_diagonal(bds[0], 1, 1)
            pool.tensor_copy(ID[:, :], bds[0]).then_inc(id_ok, 1)
            pool.wait_ge(id_ok, 1)
            for i in range(1, 7):
                block_diagonal(bds[i], 1 << i, 1 << i)
            block_diagonal(BDG[:, :], 64, 128)
            signal(pool.tensor_copy(BD[:, :], bds[6]))
            signal(pool.memset(ONES[:, :], 1.0))
            signal(pool.memset(RM[:, :], 1.0))
            link(pool.affine_select(out=SU[:, :], in_=ones, compare_op=ALU.is_gt, fill=0.0, base=0,
                                    pattern=[[1, P]], channel_multiplier=-1))
            link(pool.affine_select(out=SL[:, :], in_=ones, compare_op=ALU.is_gt, fill=0.0, base=0,
                                    pattern=[[-1, P]], channel_multiplier=1))
            link(pool.memset(RM[:, :].rearrange("p (c t) -> p c t", c=NCH)[:, :, 0:1], 0.0))
            link(pool.tensor_tensor(SL[:, :], SL[:, :], BD[:, :], ALU.mult))
            link(pool.tensor_tensor(MK[:, 0:P], SU[:, :], BD[:, :], ALU.mult))
            link(pool.tensor_tensor(MK[:, P:2 * P], MK[:, 0:P], ID[:, :], ALU.add))
            link(pool.tensor_copy(MK[:, 2 * P:4 * P], MK[:, 0:2 * P]))
            link(pool.tensor_tensor(D1L[:, :], bds[1], bds[0], ALU.subtract))
            link(pool.tensor_tensor(D1U[:, :], D1L[:, :], SU[:, :], ALU.mult))
            link(pool.tensor_tensor(D1L[:, :], D1L[:, :], SL[:, :], ALU.mult))
            for i in range(5):
                d = DL[:, P * i:P * (i + 1)]
                link(pool.tensor_tensor(d, bds[i + 2], bds[i + 1], ALU.subtract))
                link(pool.tensor_tensor(d, d, SL[:, :], ALU.mult))
            link(pool.iota(IOTA[:, :], pattern=[[0, 2], [1, SLOTS]], base=0, channel_multiplier=0,
                           allow_small_or_imprecise_dtypes=True))
            pool.memset(POSB[:, :], -5.0).then_inc(masks, 1)
            pool.wait_ge(masks, 1)
            pool.memset(OHGT[:, :], 0.0).then_inc(masks, 1)
            pool.wait_ge(masks, 2)
            pool.memset(RT[:, :], NEG).then_inc(masks, 1)
            pool.wait_ge(masks, 3)
            pool.memset(GATES[:, :], 0.0).then_inc(masks, 1)

            xg, ab, la, bs = GLT
            pool.wait_ge(gx_ok, 1)
            link(pool.tensor_scalar(xg, xg, 0.0, None, ALU.min))
            pool.wait_ge(gln_ok, 1)
            link(pool.tensor_tensor(la, xg, ab, ALU.subtract), gla_la)
            pool.wait_ge(gb_ok, 1)
            b4 = bs.rearrange("p (h c t) -> p h c t", h=2, c=NCH)
            d4 = la.rearrange("p (h c t) -> p h c t", h=2, c=NCH)
            mid, last = b4[:, :, :, L // 2 - 1:L // 2], b4[:, :, :, L - 1:L]
            for h in range(2):
                signal(pool.tensor_tensor(d4[:, h], b4[:, h], mid[:, h].broadcast_to([P, NCH, L]), ALU.subtract))
            em3 = EM[:, :].rearrange("p (w h c) -> p w h c", w=3, h=2)
            signal(pool.tensor_copy(em3[:, 0], mid.rearrange("p h c o -> p h (c o)")))
            signal(pool.tensor_tensor(em3[:, 1], last.rearrange("p h c o -> p h (c o)"), mid.rearrange("p h c o -> p h (c o)"), ALU.subtract))
            signal(pool.tensor_copy(em3[:, 2], last.rearrange("p h c o -> p h (c o)")))
            settle()
            pool.memset(SM[:, 120:121], 0.0).then_inc(gdiff, 1)
            pool.wait_ge(gdiff, 1)
            pool.wait_ge(gexp, 3)
            g4 = GQK[:, :].rearrange("p (h t) -> p h t", h=4)
            ep, en = xg.rearrange("p (h t) -> p h t", h=2), ab.rearrange("p (h t) -> p h t", h=2)
            link(pool.tensor_scalar(ep, ep, float(GQ // GH) ** -0.5, None, ALU.mult))
            signal(pool.tensor_tensor(QE, g4[:, 0:2], ep, ALU.mult))
            link(pool.tensor_tensor(KE, g4[:, 2:4], en, ALU.mult))
            for h in range(2):
                def c3(a):
                    return a[:, h].rearrange("p (c t) -> p c t", c=NCH)
                signal(pool.tensor_tensor(c3(QB), c3(QE), em3[:, 0, h].unsqueeze(2).broadcast_to([P, NCH, L]), ALU.mult))
                signal(pool.tensor_tensor(c3(KL), c3(KE), em3[:, 1, h].unsqueeze(2).broadcast_to([P, NCH, L]), ALU.mult))
            settle()
            pool.memset(SM[:, 121:122], 0.0).then_inc(gla_el, 1)
            pool.wait_ge(gla_el, 1)
            pool.wait_ge(rows_in, 48)
            pool.wait_ge(gsig, 1)
            gg3 = GG.rearrange("p (t w) -> p t w", t=TT)
            link(pool.tensor_tensor(GG, GG, GSIG, ALU.mult))
            pool.tensor_tensor(gg3, gg3, ROWS[:, 2:3, :].broadcast_to([P, TT, 512]), ALU.mult).then_inc(ggn, 1)
            pool.wait_ge(bon_ok, 1)
            pool.wait_ge(tok_v, 4)
            pool.wait_ge(tok_a, 4)
            pool.tensor_tensor(GTMP.rearrange("p (g d) -> p g d", d=L), Vt.rearrange("p (g d) -> p g d", d=L),
                               BON[:, :].unsqueeze(2).broadcast_to([P, 16, L]), ALU.mult).then_inc(bv_ok, 1)

        @block.scalar
        def _(act):
            signal, settle, link = linker(act, ach)

            def square_sums(n, src, junk):
                for t in range(TT):
                    link(act.activation(junk, src[:, t, :], ACT.Square, accum_out=SM[:, 4 * n + t:4 * n + t + 1]))
                act.activation(SM[:, 4 * n + 2:4 * n + 4], SM[:, 4 * n:4 * n + 2], ACT.Sqrt, bias=EPS, scale=1.0 / D
                               ).then_inc(rstd_sq, 1)

            act.wait_ge(x_in, 16)
            square_sums(0, XB3, T34[:, 1024:2048])
            act.wait_ge(vec_t, 1)
            act.activation(VC[:, 0:NV], bank(7)[:, 0:NV], ACT.Copy).then_inc(vc_ok, 1)
            act.wait_ge(vc_ok, 1)
            link(act.activation(OMU[:, 0:14], col("shift_mu", 0, 14), ACT.Copy, scale=-1.0, bias=1.0))
            link(act.activation(OMKA[:, 0:4], col("rw_ka", 0, 4), ACT.Copy, scale=-1.0, bias=1.0), vc_ok)

            def transposed(n, gain):
                for k in (0, 1, 4, 5):
                    act.wait_ge(xt_ps, KC * n + 2 * (k // 2) + 2)
                    src = PS[:, (0 if n < 3 else 4 * BANK) + 256 * k:(0 if n < 3 else 4 * BANK) + 256 * (k + 1)]
                    if gain:
                        act.activation(UT3[:, k, :], src, ACT.Copy, scale=col(gain, k)).then_inc(ut_a, 1)
                    else:
                        act.activation(UT3[:, k, :], src, ACT.Copy).then_inc(ut_a, 1)

            transposed(0, "norm_mix")

            tile_dst = [L1, L2] + [KR[:, 256 * i:256 * (i + 1)] for i in range(4)] + [RR[:, 256 * i:256 * (i + 1)] for i in range(4)] \
                + [T4[:, 256 * i:256 * (i + 1)] for i in range(4)]
            mu_at = [12, 13] + [4, 5, 6, 7] + [0, 1, 2, 3] + [8, 9, 10, 11]

            def shift_half(n):
                act.wait_ge(tile_ps, n + 1)
                if n == 10:
                    act.wait_ge(masks, 1)
                act.activation(tile_dst[n], PS[:, (4 + n % 4) * BANK:(4 + n % 4) * BANK + T], ACT.Copy,
                               scale=OMU[:, mu_at[n]:mu_at[n] + 1]).then_inc(tile_a, 1)

            for n in range(2):
                shift_half(n)
            act.wait_ge(tile_v, 2)
            signal(act.activation(L1[0:64, :], L1[0:64, :], ACT.Tanh), lora_act)
            signal(act.activation(L2, L2, ACT.Sigmoid), lora_act)
            for n in range(2, 6):
                shift_half(n)
            act.wait_ge(z_ps, 1)
            act.wait_ge(xt_ps, KC)
            for h in range(HP):
                act.activation(T1[:, 256 * h:256 * (h + 1)], PS[:, 256 * h:256 * (h + 1)], ACT.Sigmoid,
                               bias=col("rw_w0", h)).then_inc(sz_ok, 1)
            act.wait_ge(a_ps, 1)
            for h in range(HP):
                act.activation(T2[:, 256 * h:256 * (h + 1)], PS[:, 1024 + 256 * h:1024 + 256 * (h + 1)], ACT.Sigmoid,
                               bias=col("rw_a0", h)).then_inc(iclr_ok, 1)
            for n in range(6, 14):
                shift_half(n)
            act.wait_ge(ss_max, 1)
            act.activation(BF, BF, ACT.Sqrt).then_inc(nrm_ok, 1)
            for i in range(5):
                n = 14 + i
                act.wait_ge(tile_ps, n + 1)
                dst = GQK[:, 256 * i:256 * (i + 1)] if i < 4 else DGK[0:16, :]
                m = P if i < 4 else 16
                act.activation(dst, PS[0:m, (4 + n % 4) * BANK:(4 + n % 4) * BANK + T], ACT.Copy).then_inc(tile_g, 1)
            act.wait_ge(cs_ok, 1)
            act.activation(AR5[:, :, :, 0, :], T1.rearrange("p (h t c) -> p h t c", h=HP, t=TT), ACT.Exp, scale=-DECAY).then_inc(exp_ok, 1)
            act.wait_ge(exp_used, 1)
            act.activation(T1, T3, ACT.Exp, scale=DECAY).then_inc(exp_ok, 1)
            act.wait_ge(gv_ps, 1)
            for t in range(TT):
                signal(act.activation(GV[:, 512 * t:512 * (t + 1)], bank(2 + t), ACT.Copy), gvg_ok)
            act.wait_ge(gg_ps, 1)
            for t in range(TT):
                signal(act.activation(GG[:, 512 * t:512 * (t + 1)], bank(0 + t), ACT.Copy), gvg_ok)
            xg, ab, la, bs = GLT
            act.wait_ge(gk_ps, 1)
            act.wait_ge(tile_ps, 18)
            for h in range(2):
                src = bank(7)[:, 256 * h:256 * (h + 1)]
                signal(act.activation(xg[:, 256 * h:256 * (h + 1)], src, ACT.Identity, bias=col("gla_gk_b", h)))
            for h in range(2):
                src = bank(7)[:, 256 * h:256 * (h + 1)]
                signal(act.activation(ab[:, 256 * h:256 * (h + 1)], src, ACT.Abs, bias=col("gla_gk_b", h)), gk_read)
            settle()
            act.wait_ge(exp_used, 2)
            act.activation(T1, T3, ACT.Exp, scale=-DECAY).then_inc(exp_ok, 1)
            for i, (grp, dst) in enumerate(((0, Vt), (1, Vt), (4, Bt), (5, Bt))):
                act.wait_ge(tok_ps, grp + 1)
                act.activation(dst[:, 512 * (i % 2):512 * (i % 2 + 1)], bank(grp), ACT.Copy).then_inc(tok_a, 1)
            act.wait_ge(gk_read, 2)
            act.activation(ab, ab, ACT.Exp, scale=-1.0).then_inc(gx_ok, 1)
            act.wait_ge(gx_ok, 1)
            act.activation(ab, ab, ACT.Ln, bias=1.0).then_inc(gln_ok, 1)
            act.wait_ge(gdiff, 1)
            act.activation(xg, la, ACT.Exp, scale=1.0 / TEMP).then_inc(gexp, 1)
            act.activation(ab, la, ACT.Exp, scale=-1.0 / TEMP).then_inc(gexp, 1)
            act.activation(EM[:, :], EM[:, :], ACT.Exp, scale=1.0 / TEMP).then_inc(gexp, 1)
            act.wait_ge(gvg_ok, 4)
            act.wait_ge(mat_ok, 8)
            act.activation(GSIG, GG, ACT.Sigmoid).then_inc(gsig, 1)
            for g in range(4):
                act.wait_ge(mv_ps, g + 1)
                act.activation(AY4[:, g // 2, 4 * (g % 2):4 * (g % 2) + 4, 64:128],
                               bank(2 * g)[:, 0:256].rearrange("p (h w) -> p h w", h=4), ACT.Copy).then_inc(mv_ok, 1)
            act.wait_ge(klt_ps, 1)
            act.activation(KLT, bank(4).rearrange("p (t h w) -> p t h w", t=TT, h=2), ACT.Copy).then_inc(klt_ok, 1)
            act.wait_ge(go_ps, 1)
            act.activation(T34[:, 0:1024], bank(2, 2), ACT.Square).then_inc(osq_a, 1)
            act.wait_ge(ovar, 1)
            act.activation(SM[:, 48:56], SM[:, 40:48], ACT.Sqrt, bias=EPS, scale=1.0 / 128).then_inc(orstd, 1)
            act.wait_ge(osq_v, 1)
            act.activation(T34[:, 0:1024], KRR[:, 0:1024], ACT.Square).then_inc(osq_a, 1)
            act.wait_ge(ovar, 2)
            act.activation(SM2[:, 32:48], SM2[:, 16:32], ACT.Sqrt, bias=GN_EPS, scale=1.0 / L).then_inc(orstd, 1)
            act.wait_ge(y_rw, 1)
            act.wait_ge(y_gla, 1)
            transposed(1, None)
            act.wait_ge(wout_ps, 1)
            act.wait_ge(scaled, 2)
            square_sums(2, XB3, T34[:, 1024:2048])
            transposed(2, "norm_ffn")
            act.wait_ge(lg_max, 1)
            for t in range(TT):
                act.activation(RT8[1][:, t, 0:NE], RT8[0][:, t, 0:NE], ACT.Exp, bias=SM[:, 100 + t:101 + t]).then_inc(lg_exp, 1)
            act.wait_ge(gtt_ps, 1)
            act.activation(GT[0:NE, :], bank(6)[0:NE, 0:T], ACT.Copy).then_inc(gt_ok, 1)
            act.wait_ge(cnt_ok, 1)

            def item(i):
                act.wait_ge(h0_ps, i + 1)
                act.activation(HS[:, 0:512], bank(4), ACT.Copy).then_inc(hs0, 1)
                act.wait_ge(ohgt_ps, i + 1)
                act.wait_ge(scattered, i + 1)
                act.activation(OHGT[:, :], bank(7)[:, 0:T], ACT.Copy).then_inc(ohgt_ok, 1)
                for g in range(2):
                    act.wait_ge(glu_ok, i * 2 + (g + 1))
                    act.activation(SIG[:, 4 * g:4 * g + 4], GLU[:, 4 * g:4 * g + 4], ACT.Sigmoid, scale=1.702).then_inc(sig_ok, 1)
                act.wait_ge(w2_used, i * 4 + 4)
                act.activation(YS, bank(7), ACT.Copy).then_inc(ys_ok, 1)

            def experts(nb):
                with act.Fori(0, NE) as e:
                    for b in range(nb):
                        item(e * nb + b)

            most = act.value_load(CNTI[0:1, 0:1], min_val=0, max_val=T)
            with act.If(most > SLOTS):
                experts(NBMAX)
            with act.Else():
                experts(1)
            act.wait_ge(scaled, 4)
            square_sums(3, XB3, T34[:, 1024:2048])
            act.wait_ge(pt_ps, 1)
            act.activation(PT, bank(4).rearrange("p (k t) -> p k t", k=2), ACT.Copy).then_inc(pt_ok, 1)
            transposed(3, "norm_ple")
            act.wait_ge(pg_ps, 1)
            act.activation(ZG, bank(0, 4), ACT.Sigmoid).then_inc(psig, 1)
            act.wait_ge(scaled, 6)
            square_sums(4, XB3, T34[:, 1024:2048])

        @block.vector
        def _(dve):
            signal, settle, link = linker(dve, vch)

            def scale_rows(n, dst):
                dve.wait_ge(rstd_sq, n + 1 if n < 2 else n)
                link(dve.reciprocal(SM[:, 20 + 2 * n:22 + 2 * n], SM[:, 4 * n + 2:4 * n + 4]))
                for t in range(TT):
                    signal(dve.tensor_scalar(dst[:, t, :], XB3[:, t, :], SM[:, 20 + 2 * n + t:21 + 2 * n + t], None, ALU.mult), scaled)

            def transposed(n, gain):
                for k in (2, 3, 6, 7):
                    dve.wait_ge(xt_ps, KC * n + 2 * (k // 2) + 2)
                    src = PS[:, (0 if n < 3 else 4 * BANK) + 256 * k:(0 if n < 3 else 4 * BANK) + 256 * (k + 1)]
                    if gain:
                        dve.tensor_scalar(UT3[:, k, :], src, col(gain, k), None, ALU.mult).then_inc(ut_v, 1)
                    else:
                        dve.tensor_copy(UT3[:, k, :], src).then_inc(ut_v, 1)

            dve.wait_ge(x_in, 16)
            dve.wait_ge(rstd_sq, 1)
            link(dve.reciprocal(SM[:, 20:22], SM[:, 2:4]))
            for t in range(TT):
                dve.tensor_scalar(XB3[:, t, :], XB3[:, t, :], SM[:, 20 + t:21 + t], None, ALU.mult).then_inc(xs_ok, 1)
            dve.wait_ge(vc_ok, 1)
            transposed(0, "norm_mix")

            tile_dst = [L1, L2] + [KR[:, 256 * i:256 * (i + 1)] for i in range(4)] + [RR[:, 256 * i:256 * (i + 1)] for i in range(4)] \
                + [T4[:, 256 * i:256 * (i + 1)] for i in range(4)]
            mu_at = [12, 13] + [4, 5, 6, 7] + [0, 1, 2, 3] + [8, 9, 10, 11]

            def shift(n):
                dve.wait_ge(tile_a, n + 1)
                src = PS[:, (4 + n % 4) * BANK:(4 + n % 4) * BANK + T - 1]
                d = tile_dst[n][:, 1:T]
                dve.scalar_tensor_tensor(out=d, in0=src, scalar=col("shift_mu", mu_at[n]), in1=d, op0=ALU.mult,
                                         op1=ALU.add).then_inc(tile_v, 1)

            for n in range(6):
                shift(n)
            dve.wait_ge(tile_v, 6)
            for h in range(HP):
                signal(dve.tensor_scalar(hp3(KF)[:, h], hp3(KR)[:, h], col("rw_kk", h), None, ALU.mult))
            settle()
            link(dve.tensor_tensor(BF, KF, KF, ALU.mult), sq_ok)
            for n in range(6, 10):
                shift(n)
            dve.wait_ge(iclr_ok, 4)
            dve.wait_ge(masks, 1)
            for h in range(HP):
                signal(dve.tensor_scalar(hp3(T3)[:, h], hp3(T2)[:, h], col("rw_ka", h), OMKA[:, h:h + 1], ALU.mult, ALU.add))
            settle()
            link(dve.tensor_tensor(KR, KR, T3, ALU.mult))
            dve.wait_ge(sz_ok, 4)
            dve.wait_ge(masks, 1)
            for h in range(HP):
                signal(dve.tensor_tensor_scan(out=hp3(T3)[:, h], data0=RM[:, :], data1=hp3(T1)[:, h], initial=0.0,
                                              op0=ALU.mult, op1=ALU.add))
            settle()
            for n in range(10, 14):
                shift(n)
            link(dve.tensor_tensor(T1, T3, T1, ALU.subtract), cs_ok)
            dve.wait_ge(ss_ps, 1)
            link(dve.tensor_scalar(BF, bank(0, 2), 1e-24, None, ALU.max), ss_max)
            dve.wait_ge(nrm_ok, 1)
            link(dve.reciprocal(BF, BF))
            link(dve.tensor_tensor(KF, KF, BF, ALU.mult))
            dve.wait_ge(exp_ok, 1)
            kf4 = KF.rearrange("p (h t c) -> p h t c", h=HP, t=TT)
            for h in range(HP):
                signal(dve.scalar_tensor_tensor(out=AR5[:, h, :, 0, :], in0=AR5[:, h, :, 0, :], scalar=-1.0, in1=kf4[:, h],
                                                op0=ALU.mult, op1=ALU.mult), a_ok)
            signal(dve.tensor_tensor(BF, KF, T2, ALU.mult), exp_used)
            settle(exp_used)
            settle(a_ok)
            dve.wait_ge(exp_ok, 2)
            signal(dve.tensor_tensor(KF, KR, T1, ALU.mult), kf_ok)
            link(dve.tensor_tensor(BF, BF, T1, ALU.mult), exp_used)
            dve.wait_ge(exp_ok, 3)
            r4, t4 = RR.rearrange("p (h t c) -> p h t c", h=HP, t=TT), T1.rearrange("p (h t c) -> p h t c", h=HP, t=TT)
            signal(dve.tensor_copy(PLC[:, :], T1.rearrange("p (g c) -> p g c", c=L)[:, :, L - 1]))
            for h in range(HP):
                signal(dve.tensor_tensor(AR5[:, h, :, 1, :], r4[:, h], t4[:, h], ALU.mult))
            link(dve.tensor_tensor(T2, RR, KR, ALU.mult), r_ok)
            for h in range(HP):
                signal(dve.tensor_scalar(hp3(T2)[:, h], hp3(T2)[:, h], col("rw_rk", h), None, ALU.mult))
            settle()
            dve.memset(SM[:, 122:123], 0.0).then_inc(rkk_ok, 1)
            for i, grp in enumerate((2, 3)):
                dve.wait_ge(tok_ps, grp + 1)
                dve.tensor_copy(Kt[:, 512 * i:512 * (i + 1)], bank(grp)).then_inc(tok_v, 1)
            for i, grp in enumerate((6, 7)):
                dve.wait_ge(tok_ps, grp + 1)
                dve.tensor_copy(AY4[:, i, :, 0:64], bank(grp).rearrange("p (h w) -> p h w", h=NH)).then_inc(tok_v, 1)
            dve.wait_ge(bon_ps, 1)
            dve.tensor_copy(BON[:, :], bank(2)[:, 0:16]).then_inc(bon_ok, 1)
            dve.wait_ge(gg_ps, 1)
            dve.wait_ge(masks, 1)
            mk1 = MK[:, :]
            for u in range(8):
                t, h = u // 4, u % 4
                b0 = 4 * (u % 2)
                dve.wait_ge(mat_ps, u + 1)
                for j in range(2):
                    m = 8 * t + 2 * h + j
                    signal(dve.tensor_tensor(MT[:, m, :], bank(b0 + j), mk1, ALU.mult))
                    signal(dve.tensor_tensor(TAB[:, m, :], bank(b0 + 2 + j)[:, 0:P], SL[:, :], ALU.mult))
                settle()
                dve.memset(SM[:, 123:124], 0.0).then_inc(mat_ok, 1)
                dve.wait_ge(mat_ok, u + 1)
                if u == 0:
                    dve.wait_ge(gla_la, 1)
                    for q in range(2):
                        signal(dve.tensor_tensor_scan(out=GLT[3][:, 256 * q:256 * (q + 1)], data0=RM[:, :],
                                                      data1=GLT[2][:, 256 * q:256 * (q + 1)], initial=0.0,
                                                      op0=ALU.mult, op1=ALU.add))
                    settle()
                    dve.memset(SM[:, 124:125], 0.0).then_inc(gb_ok, 1)
                    dve.wait_ge(gb_ok, 1)
            for src, m1, dst, s in ((TAB, D1L, X_, x1_ok), (MT[:, :, 0:P], D1U, XT_, x1t_ok)):
                for q in range(2):
                    link(dve.tensor_tensor(dst[:, 8 * q:8 * q + 8, :], src[:, 8 * q:8 * q + 8, :],
                                           m1[:, :].unsqueeze(1).broadcast_to([P, 8, P]), ALU.mult))
                    link(dve.tensor_tensor(dst[:, 8 * q:8 * q + 8, :], dst[:, 8 * q:8 * q + 8, :],
                                           ID[:, :].unsqueeze(1).broadcast_to([P, 8, P]), ALU.add), s)
            dve.wait_ge(gla_el, 1)
            for lv in range(5):
                for g in range(4):
                    dve.wait_ge(y_ps, 4 * lv + g + 1)
                    link(dve.tensor_tensor(Y_[:, 4 * g:4 * g + 4, :], bank(2 * g).rearrange("p (m w) -> p m w", m=4),
                                           DL[:, P * lv:P * (lv + 1)].unsqueeze(1).broadcast_to([P, 4, P]), ALU.mult), y_ok)
                for g in range(4):
                    dve.wait_ge(xx_ps, 4 * lv + g + 1)
                    signal(dve.tensor_tensor(X_[:, 4 * g:4 * g + 4, :], bank(2 * g + 1).rearrange("p (m w) -> p m w", m=4),
                                             X_[:, 4 * g:4 * g + 4, :], ALU.add), xx_ok)
                    link(dve.tensor_tensor(XT_[:, 4 * g:4 * g + 4, :], bank(2 * g).rearrange("p (m w) -> p m w", m=4),
                                           XT_[:, 4 * g:4 * g + 4, :], ALU.add), xx_ok)
            for g in range(4):
                dve.wait_ge(wu_ps, g + 1)
                dve.tensor_copy(WU[:, :, g // 2, 4 * (g % 2):4 * (g % 2) + 4, :].rearrange("p w h d -> p h w d"),
                                bank(2 * g + 1).rearrange("p (h w d) -> p h w d", h=4, w=2)).then_inc(wu_ok, 1)
            for t in range(TT):
                dve.wait_ge(reff_ps, t + 1)
                dve.tensor_tensor(REFF[:, t], bank(t).rearrange("p (h w) -> p h w", h=HP), AR5[:, :, t, 1, :], ALU.add).then_inc(reff_ok, 1)
            hb = (2, 5, 3)
            gb = (6, 4)
            bdb = BD[:, :].unsqueeze(1).broadcast_to([P, HP, P])

            def h4(a):
                return a.rearrange("p (h w) -> p h w", h=HP)

            for c in range(3):
                dve.wait_ge(h_ps, c + 1)
                signal(dve.tensor_tensor(h4(HS_[:, c]), h4(bank(hb[c])), bdb, ALU.mult))
            for c in range(2):
                dve.wait_ge(gt_ps, c + 1)
                signal(dve.tensor_tensor(GTS[:, c], h4(bank(gb[c])), bdb, ALU.mult))
            settle()

            def pl(c):
                return PLC[:, :].rearrange("p (h c) -> p h c", h=HP)[:, :, c:c + 1].broadcast_to([P, HP, P])

            link(dve.tensor_tensor(SRW[:, 0], h4(HS_[:, 0]), pl(0), ALU.mult), st_ok)
            for c in (1, 2):
                dve.wait_ge(st_ps, c)
                link(dve.tensor_tensor(HS_[:, c], bank(7 if c == 1 else 2), HS_[:, c], ALU.add))
                link(dve.tensor_tensor(SRW[:, c], h4(HS_[:, c]), pl(c), ALU.mult), st_ok)

            for t in range(TT):
                dve.wait_ge(att_ps, t + 1)
                for j in range(2):
                    b = 5 + j
                    link(dve.tensor_tensor(ATT[:, t, j:GH:2, :], bank(b)[:, 0:256].rearrange("p (h w) -> p h w", h=2),
                                           MK[:, P:2 * P].unsqueeze(1).broadcast_to([P, 2, P]), ALU.mult), att_ok)
            sgt = T34[:, 0:512]
            em3 = EM[:, :].rearrange("p (w h c) -> p w h c", w=3, h=2)
            for c in range(3):
                dve.wait_ge(sg_ps, c + 1)
                dst = SG if c == 0 else sgt
                if c:
                    dve.wait_ge(go_used, c)
                s2 = SG.rearrange("p (h w) -> p h w", h=2)
                ins = dve.tensor_tensor(dst.rearrange("p (h w) -> p h w", h=2), bank(7).rearrange("p (h w) -> p h w", h=2),
                                        BDG[:, :].unsqueeze(1).broadcast_to([P, 2, 256]), ALU.mult)
                if c == 0:
                    link(ins, sg_ok)
                else:
                    signal(ins)
                    link(dve.tensor_tensor(s2, s2, em3[:, 2, :, c:c + 1].broadcast_to([P, 2, 256]), ALU.mult))
                    link(dve.tensor_tensor(SG, SG, sgt, ALU.add), sg_ok)
            dve.wait_ge(osq_a, 1)
            link(dve.tensor_reduce(SM[:, 40:48], T34[:, 0:1024].rearrange("p (g w) -> p g w", g=8), AX.X, ALU.add), ovar)
            dve.wait_ge(orstd, 1)
            link(dve.reciprocal(SM[:, 56:64], SM[:, 48:56]))
            dve.wait_ge(ggn, 1)
            yg = YT[:, :, 512:1024]
            for t in range(TT):
                signal(dve.tensor_tensor(yg[:, t].rearrange("p (h w) -> p h w", h=GH), bank(2 + t).rearrange("p (h w) -> p h w", h=GH),
                                         SM[:, 56 + 4 * t:60 + 4 * t].unsqueeze(2).broadcast_to([P, GH, P]), ALU.mult))
            settle()
            link(dve.tensor_tensor(yg, yg, GG.rearrange("p (t w) -> p t w", t=TT), ALU.mult), y_gla)
            dve.wait_ge(o_ps, 1)
            oc = KRR[:, 0:1024]
            og = oc.rearrange("p (g d) -> p g d", d=L)
            ob = bank(0, 2).rearrange("p (g d) -> p g d", d=L)
            link(dve.tensor_reduce(SM2[:, 0:16], ob, AX.X, ALU.add))
            link(dve.tensor_scalar(SM2[:, 0:16], SM2[:, 0:16], 1.0 / L, None, ALU.mult))
            link(dve.tensor_tensor(og, ob, SM2[:, 0:16].unsqueeze(2).broadcast_to([P, 16, L]), ALU.subtract), osq_v)
            dve.wait_ge(osq_a, 2)
            link(dve.tensor_reduce(SM2[:, 16:32], T34[:, 0:1024].rearrange("p (g d) -> p g d", d=L), AX.X, ALU.add), ovar)
            dve.wait_ge(orstd, 2)
            link(dve.reciprocal(SM2[:, 48:64], SM2[:, 32:48]))
            link(dve.tensor_tensor(og, og, SM2[:, 48:64].unsqueeze(2).broadcast_to([P, 16, L]), ALU.mult))
            o3 = oc.rearrange("p (t w) -> p t w", t=TT)
            dve.wait_ge(rows_in, 48)
            link(dve.tensor_tensor(o3, o3, ROWS[:, 0:1, :].broadcast_to([P, TT, 512]), ALU.mult))
            link(dve.tensor_tensor(o3, o3, ROWS[:, 1:2, :].broadcast_to([P, TT, 512]), ALU.add))
            dve.wait_ge(bv_ok, 1)
            link(dve.tensor_tensor(oc, oc, GTMP, ALU.add))
            dve.wait_ge(gate_ps, 1)
            link(dve.tensor_tensor(YT[:, :, 0:512], bank(5, 2).rearrange("p (t w) -> p t w", t=TT), o3, ALU.mult), y_rw)
            transposed(1, None)
            dve.wait_ge(wout_ps, 1)
            dve.wait_ge(x_in, 32)
            for t in range(TT):
                if t:
                    dve.wait_ge(wout_used, 1)
                signal(dve.tensor_tensor(XB3[:, t, :], bank(4 + 2 * t, 2), XB3[:, t, :], ALU.add), scaled)
            settle(scaled)
            dve.wait_ge(rstd_sq, 2)
            link(dve.reciprocal(SM[:, 24:26], SM[:, 10:12]))
            for t in range(TT):
                signal(dve.tensor_scalar(U2[:, t, :], XB3[:, t, :], SM[:, 24 + t:25 + t], None, ALU.mult), u2_ok)
            transposed(2, "norm_ffn")
            dve.wait_ge(masks, 4)
            dve.wait_ge(lg_ps, 1)
            lg, ex, mr, ms, top = RT8[0], RT8[1], RT8[2], RT8[3], RT8[4]
            link(dve.tensor_copy(lg[:, :, 0:NE], bank(6)[:, 0:TT * NE].rearrange("p (t e) -> p t e", t=TT)))
            for t in range(TT):
                signal(dve.max(top[:, t, 0:8], lg[:, t, 0:NE + 4]))
            settle()
            link(dve.tensor_scalar(SM[:, 100:102], top[:, :, 0:1].rearrange("p t o -> p (t o)"), -1.0, None, ALU.mult), lg_max)
            link(dve.memset(top[:, :, 4:8], NEG))
            for t in range(TT):
                signal(dve.match_replace(mr[:, t, 0:NE + 4], top[:, t, 0:8], lg[:, t, 0:NE + 4], 2 * NEG))
            settle()
            signal(dve.tensor_tensor(ms[:, :, 0:NE], mr[:, :, 0:NE], lg[:, :, 0:NE], ALU.not_equal), sel_ok)
            settle(sel_ok)
            dve.wait_ge(lg_exp, 2)
            link(dve.tensor_tensor(ex[:, :, 0:NE], ex[:, :, 0:NE], ms[:, :, 0:NE], ALU.mult))
            link(dve.tensor_reduce(SM[:, 104:106], ex[:, :, 0:NE], AX.X, ALU.add))
            link(dve.reciprocal(SM[:, 106:108], SM[:, 104:106]))
            link(dve.tensor_tensor(GAT3[:, :, 0:NE], ex[:, :, 0:NE], SM[:, 106:108].unsqueeze(2).broadcast_to([P, TT, NE]), ALU.mult), gates_ok)
            dve.wait_ge(pos_ps, 1)
            pp = RT8[5]
            link(dve.scalar_tensor_tensor(out=pp[:, :, 0:NE], in0=bank(7)[:, 0:TT * NE].rearrange("p (t e) -> p t e", t=TT),
                                          scalar=1.0, in1=ms[:, :, 0:NE], op0=ALU.add, op1=ALU.mult))
            for b in range(NBMAX):
                signal(dve.tensor_scalar(POS4[:, b, :, 0:NE], pp[:, :, 0:NE], -1.0 - SLOTS * b, None, ALU.add))
            signal(dve.tensor_reduce(CMAX[:, :], bank(7)[:, 64:96], AX.X, ALU.max))
            settle()
            link(dve.tensor_copy(CNTI[:, :], CMAX[:, :]), cnt_ok)
            dve.wait_ge(b1_ps, 1)
            link(dve.tensor_copy(B1T.rearrange("p e c g -> p g c e"), bank(5).rearrange("p (g c e) -> p g c e", g=2, c=8)), b1_ok)
            dve.memset(YS, 0.0).then_inc(ys_ok, 1)

            def one_hot(b, e):
                for t in range(TT):
                    ins = dve.tensor_scalar(OH3[:, t, :], IOTA[:, 0:SLOTS], POS4[:, b, t, bass.ds(e, 1)], None, ALU.is_equal)
                    if t == TT - 1:
                        ins.then_inc(oh_ok, 1)

            def gather_evac():
                dve.tensor_tensor(XG, bank(6).rearrange("p (k s) -> p k s", k=KC),
                                  col("norm_ffn", 0, 8).unsqueeze(2).broadcast_to([P, KC, SLOTS]), ALU.mult).then_inc(xg_ok, 1)

            one_hot(0, 0)
            dve.wait_ge(gathered, 1)
            gather_evac()

            def item(i, b, e, nb_, ne_):
                for t in range(TT):
                    ins = dve.tensor_scalar(OHG3[:, t, :], IOTA[:, :], POS4[:, b, t, bass.ds(e, 1)], GAT3[:, t, bass.ds(e, 1)],
                                            ALU.is_equal, ALU.mult)
                    if t == TT - 1:
                        ins.then_inc(ohg_ok, 1)
                one_hot(nb_, ne_)
                dve.wait_ge(w1_used, i * KC + KC)
                dve.tensor_copy(HS[:, 512:1024], bank(5)).then_inc(hs1, 1)
                for g in range(2):
                    cs = slice(4 * g, 4 * g + 4)
                    dve.wait_ge(t_ps, i * 2 + (g + 1))
                    dve.tensor_tensor(TP[:, cs].rearrange("p c (g s) -> p c g s", g=2),
                                      bank(4 + g).rearrange("p (c g s) -> p c g s", c=4, g=2),
                                      B1T[:, bass.ds(e, 1), cs, :].rearrange("p e c g -> p (e c) g").unsqueeze(3).broadcast_to([P, 4, 2, SLOTS]),
                                      ALU.add).then_inc(t_ok, 1)
                    dve.wait_ge(t_ok, i * 2 + (g + 2))
                    dve.tensor_scalar(GLU[:, cs], TP[:, cs, 0:SLOTS], 7.0, None, ALU.min).then_inc(glu_ok, 1)
                    dve.tensor_scalar(LIN[:, cs], TP[:, cs, SLOTS:P], 7.0, -7.0, ALU.min, ALU.max).then_inc(lin_ok, 1)
                    dve.wait_ge(glu_ok, i * 2 + (g + 1))
                    dve.wait_ge(lin_ok, i * 2 + (g + 1))
                    dve.scalar_tensor_tensor(out=LIN[:, cs], in0=LIN[:, cs], scalar=1.0, in1=GLU[:, cs], op0=ALU.add,
                                             op1=ALU.mult).then_inc(gl_ok, 1)
                for g in range(2):
                    cs = slice(4 * g, 4 * g + 4)
                    dve.wait_ge(gl_ok, i * 2 + (g + 1))
                    dve.wait_ge(sig_ok, i * 2 + (g + 1))
                    dve.tensor_tensor(ACTT[:, cs], LIN[:, cs], SIG[:, cs], ALU.mult).then_inc(act_ok, 1)
                dve.wait_ge(gathered, i + 2)
                gather_evac()

            def experts(nb):
                with dve.Fori(0, NE) as e:
                    for b in range(nb):
                        item(e * nb + b, b, e, (b + 1) % nb, e + (b + 1) // nb)

            dve.memset(SM[:, 125:126], 0.0).then_inc(t_ok, 1)
            most = dve.value_load(CNTI[0:1, 0:1], min_val=0, max_val=T)
            with dve.If(most > SLOTS):
                experts(NBMAX)
            with dve.Else():
                experts(1)
            dve.wait_ge(acc_done, 1)
            for t in range(TT):
                signal(dve.tensor_tensor(XB3[:, t, :], bank(2 * t, 2), XB3[:, t, :], ALU.add), scaled)
            settle(scaled)
            dve.wait_ge(rstd_sq, 3)
            link(dve.reciprocal(SM[:, 26:28], SM[:, 14:16]))
            for t in range(TT):
                signal(dve.tensor_scalar(U2[:, t, :], XB3[:, t, :], SM[:, 26 + t:27 + t], None, ALU.mult), u2_ok)
            transposed(3, "norm_ple")
            dve.wait_ge(pw_ps, 1)
            dve.wait_ge(psig, 1)
            link(dve.tensor_tensor(ZG, bank(4, 4), ZG, ALU.mult))
            for t in range(TT):
                signal(dve.tensor_tensor(XB3[:, t, :], XB3[:, t, :], ZG[:, 1024 * t:1024 * (t + 1)], ALU.add), scaled)
            settle(scaled)
            dve.wait_ge(rstd_sq, 4)
            link(dve.reciprocal(SM[:, 28:30], SM[:, 18:20]))
            dve.wait_ge(brow_in, 48)
            for t in range(TT):
                signal(dve.scalar_tensor_tensor(out=U2[:, t, :], in0=XB3[:, t, :], scalar=SM[:, 28 + t:29 + t], in1=NF,
                                                op0=ALU.mult, op1=ALU.mult))
            settle()
            dve.memset(SM[:, 126:127], 0.0).then_inc(fin, 1)

        @block.tensor
        def _(pe):
            def mm(out_, lhs, rhs, start=True, stop=True, shared=False):
                return pe.matmul(out_, lhs, rhs, start=start, stop=stop, skip_group_check=shared)

            pe.wait_ge(id_ok, 1)
            pe.wait_ge(vec_in, 16 * len(VROWS))
            pe.transpose(bank(7)[:, 0:NV], VEC[0:NV, :], ID[0:NV, 0:NV]).then_inc(vec_t, 1)

            def transposes(src, b0):
                for k in range(KC):
                    for t in range(TT):
                        ins = pe.transpose(PS[:, b0 * BANK + 256 * k + P * t:b0 * BANK + 256 * k + P * (t + 1)],
                                           src[:, t, P * k:P * (k + 1)], ID[:, :])
                    ins.then_inc(xt_ps, 1)

            pe.wait_ge(xs_ok, 2)
            transposes(XB3, 0)

            def tile(n, w):
                if n >= 4:
                    if n - 4 < 14:
                        pe.wait_ge(tile_v, n - 3)
                    else:
                        pe.wait_ge(tile_g, n - 4 - 13)
                m = w(0).shape[1]
                for k in range(KC):
                    ins = mm(PS[0:m, (4 + n % 4) * BANK:(4 + n % 4) * BANK + T], w(k), UT3[:, k, :], k == 0, k == KC - 1)
                ins.then_inc(tile_ps, 1)

            def cols(s, w):
                return RING[:, s * SLOT_F:s * SLOT_F + KC * w].rearrange("p (k n) -> p k n", k=KC)

            pe.wait_ge(ut_v, 4)
            pe.wait_ge(ut_a, 4)
            pe.wait_ge(vc_ok, 2)
            pe.wait_ge(win[0], 16)
            for i in range(2):
                tile(i, lambda k: cols(0, 256)[:, k, P * i:P * (i + 1)])
            pe.wait_ge(win[1], 16)
            for i in range(4):
                tile(2 + i, lambda k: cols(1, 512)[:, k, P * i:P * (i + 1)])
            pe.wait_ge(small_in, 16 * 7)
            pe.wait_ge(lora_act, 2)
            for h in range(HP):
                ins = mm(PS[:, 256 * h:256 * (h + 1)], LW[0:64, P * h:P * (h + 1)], L1[0:64, :])
            ins.then_inc(z_ps, 1)
            for h in range(HP):
                ins = mm(PS[:, 1024 + 256 * h:1024 + 256 * (h + 1)], LW[64:128, P * h:P * (h + 1)], L1[64:128, :])
            ins.then_inc(a_ps, 1)
            pe.wait_ge(win[2], 16)
            for i in range(4):
                tile(6 + i, lambda k: cols(3, 512)[:, k, P * i:P * (i + 1)])
            pe.wait_ge(masks, 4)
            pe.wait_ge(sq_ok, 1)
            pe.wait_ge(sz_ok, 4)
            for h in range(HP):
                ins = mm(PS[:, 256 * h:256 * (h + 1)], BD[:, :], hp3(BF)[:, h])
            ins.then_inc(ss_ps, 1)
            pe.wait_ge(win[3], 16)
            for i in range(4):
                tile(10 + i, lambda k: cols(5, 512)[:, k, P * i:P * (i + 1)])
            pe.wait_ge(win[4], 16)
            for i in range(4):
                tile(14 + i, lambda k: cols(7, 512)[:, k, P * i:P * (i + 1)])
            tile(18, lambda k: DGW[:, 16 * k:16 * (k + 1)])
            pe.wait_ge(win[5], 16)
            pe.wait_ge(iclr_ok, 4)
            for t in range(TT):
                for k in range(KC):
                    ins = mm(bank(2 + t), UT3[:, k, P * t:P * (t + 1)], cols(9, 512)[:, k, :], k == 0, k == KC - 1)
            ins.then_inc(gv_ps, 1)
            pe.wait_ge(tile_g, 5)
            for h in range(2):
                ins = mm(bank(7)[:, 256 * h:256 * (h + 1)], GK2[0:16, P * h:P * (h + 1)], DGK[0:16, :])
            ins.then_inc(gk_ps, 1)
            pe.wait_ge(ss_max, 1)
            pe.wait_ge(win[6], 16)
            pe.wait_ge(win[7], 16)
            for t in range(TT):
                for half, s in ((0, 11), (1, 0)):
                    for k in range(KC):
                        ins = mm(bank(t)[:, 256 * half:256 * (half + 1)], UT3[:, k, P * t:P * (t + 1)], cols(s, 256)[:, k, :],
                                 k == 0, k == KC - 1)
            ins.then_inc(gg_ps, 1)

            pe.wait_ge(gvg_ok, 4)
            pe.wait_ge(tile_v, 14)
            for grp in range(8):
                t = grp % 2
                if grp == 2:
                    pe.wait_ge(kf_ok, 1)
                if grp == 4:
                    pe.wait_ge(exp_used, 2)
                if grp == 6:
                    pe.wait_ge(gk_read, 2)
                for h in range(HP):
                    src = (hp3(T4)[:, h, P * t:P * (t + 1)], hp3(KF)[:, h, P * t:P * (t + 1)], hp3(BF)[:, h, P * t:P * (t + 1)],
                           AR5[:, h, t, 0, :])[grp // 2]
                    ins = pe.transpose(bank(grp)[:, P * h:P * (h + 1)], src, ID[:, :])
                ins.then_inc(tok_ps, 1)
            pe.wait_ge(rkk_ok, 1)
            pe.wait_ge(tok_v, 1)
            for t in range(TT):
                for h in range(HP):
                    ins = mm(bank(2)[:, 8 * t + 2 * h:8 * t + 2 * h + 2], hp3(T2)[:, h, P * t:P * (t + 1)], BD[:, 0:P:64])
            ins.then_inc(bon_ps, 1)

            pe.wait_ge(tok_a, 2)
            pe.wait_ge(tok_v, 2)
            pe.wait_ge(bon_ok, 1)
            for u in range(8):
                t, h = u // 4, u % 4
                b0 = 4 * (u % 2)
                if u == 1:
                    pe.wait_ge(tok_a, 4)
                    pe.wait_ge(tok_v, 4)
                if u >= 2:
                    pe.wait_ge(mat_ok, u - 1)
                for j in range(2):
                    r = slice(64 * j, 64 * j + 64)
                    mm(bank(b0 + j)[:, 0:256], hp3(BF)[r, h, P * t:P * (t + 1)], AR5[r, h, t, :, :])
                for j in range(2):
                    r = slice(64 * j, 64 * j + 64)
                    mm(bank(b0 + j)[:, 256:512], hp3(KF)[r, h, P * t:P * (t + 1)], AR5[r, h, t, :, :])
                for j in range(2):
                    r = slice(64 * j, 64 * j + 64)
                    ins = mm(bank(b0 + 2 + j)[:, 0:P], AR5[r, h, t, 0, :], hp3(BF)[r, h, P * t:P * (t + 1)])
                ins.then_inc(mat_ps, 1)

            pe.wait_ge(mat_ok, 8)
            pe.wait_ge(x1_ok, 2)
            pe.wait_ge(x1t_ok, 2)
            for lv in range(5):
                for g in range(4):
                    if lv:
                        pe.wait_ge(xx_ok, 2 * (4 * (lv - 1) + g + 1))
                    for q in range(4):
                        ins = mm(bank(2 * g)[:, P * q:P * (q + 1)], MT[:, 4 * g + q, 0:P], X_[:, 4 * g + q, :])
                    ins.then_inc(y_ps, 1)
                for g in range(4):
                    pe.wait_ge(y_ok, 4 * lv + g + 1)
                    for q in range(4):
                        mm(bank(2 * g + 1)[:, P * q:P * (q + 1)], XT_[:, 4 * g + q, :], Y_[:, 4 * g + q, :])
                    for q in range(4):
                        ins = mm(bank(2 * g)[:, P * q:P * (q + 1)], Y_[:, 4 * g + q, :], XT_[:, 4 * g + q, :])
                    ins.then_inc(xx_ps, 1)
            for g in range(4):
                t = g // 2
                pe.wait_ge(xx_ok, 2 * (16 + g + 1))
                for q in range(4):
                    h = 4 * (g % 2) + q
                    ins = mm(bank(2 * g)[:, 64 * q:64 * (q + 1)], MT[:, 4 * g + q, 256:384], Vt[:, 512 * t + 64 * h:512 * t + 64 * (h + 1)])
                ins.then_inc(mv_ps, 1)
            for g in range(4):
                pe.wait_ge(mv_ok, g + 1)
                for q in range(4):
                    ins = mm(bank(2 * g + 1)[:, P * q:P * (q + 1)], XT_[:, 4 * g + q, :], AY4[:, g // 2, 4 * (g % 2) + q, :])
                ins.then_inc(wu_ps, 1)
            pe.wait_ge(wu_ok, 4)
            for t in range(TT):
                for h in range(NH):
                    r = slice(64 * (h % 2), 64 * (h % 2) + 64)
                    ins = mm(bank(t)[r, P * (h // 2):P * (h // 2 + 1)], WM[:, t, 64 * h:64 * (h + 1)], MT[:, 8 * t + h, P:2 * P])
                ins.then_inc(reff_ps, 1)
            hb = (2, 5, 3)
            gb = (6, 4)
            for c in range(3):
                t, r = c // 2, slice(64 * (c % 2), 64 * (c % 2) + 64)
                for h in range(HP):
                    o = bank(hb[c])[:, P * h:P * (h + 1)]
                    tok = slice(512 * t + P * h, 512 * t + P * (h + 1))
                    mm(o, Bt[r, tok], U0[r, t, P * h:P * (h + 1)], True, False)
                    ins = mm(o, Kt[r, tok], Vt[r, tok], False, True)
                ins.then_inc(h_ps, 1)
            for i, c in enumerate((1, 2)):
                t, r = c // 2, slice(64 * (c % 2), 64 * (c % 2) + 64)
                for h in range(HP):
                    ins = mm(bank(gb[i])[:, P * h:P * (h + 1)], WM[r, t, P * h:P * (h + 1)], Bt[r, 512 * t + P * h:512 * t + P * (h + 1)])
                ins.then_inc(gt_ps, 1)
            for c in (1, 2):
                b = 7 if c == 1 else 2
                pe.wait_ge(st_ok, c)
                mm(bank(b), ID[:, :], SRW[:, c - 1].rearrange("p h w -> p (h w)"), True, False, True)
                for h in range(HP):
                    ins = mm(bank(b)[:, P * h:P * (h + 1)], GTS[:, c - 1, h, :], SRW[:, c - 1, h, :], False, h == HP - 1, True)
                ins.then_inc(st_ps, 1)
            pe.wait_ge(reff_ok, 2)
            for t in range(TT):
                for h in range(NH):
                    o = bank(t)[:, 64 * h:64 * (h + 1)]
                    mm(o, MT[:, 8 * t + h, P:2 * P], U0[:, t, 64 * h:64 * (h + 1)], h == 0, False, True)
                    ins = mm(o, MT[:, 8 * t + h, 384:512], Vt[:, 512 * t + 64 * h:512 * t + 64 * (h + 1)], False, False, True)
            for c in (1, 2, 3):
                t, r = c // 2, slice(64 * (c % 2), 64 * (c % 2) + 64)
                pe.wait_ge(st_ok, c)
                for h in range(HP):
                    ins = mm(bank(t)[r, P * h:P * (h + 1)], REFF[:, t, h, 64 * (c % 2):64 * (c % 2) + 64], SRW[:, c - 1, h, :],
                             False, c == 3, True)
            ins.then_inc(o_ps, 1)

            pe.wait_ge(gla_el, 1)
            for t in range(TT):
                for h in range(2):
                    ins = pe.transpose(bank(4)[:, 256 * t + P * h:256 * t + P * (h + 1)], KL[:, h, P * t:P * (t + 1)], ID[:, :])
            ins.then_inc(klt_ps, 1)
            for t in range(TT):
                if t:
                    pe.wait_ge(att_ok, 2)
                for q in range(2):
                    for j in range(2):
                        r = slice(64 * j, 64 * j + 64)
                        ins = mm(bank(5 + j)[:, P * q:P * (q + 1)], KE[r, q, P * t:P * (t + 1)], QE[r, q, P * t:P * (t + 1)])
                ins.then_inc(att_ps, 1)
            pe.wait_ge(klt_ok, 1)
            for t in range(TT):
                pe.wait_ge(att_ok, 2 * t + 2)
                for h in range(GH):
                    mm(bank(2 + t)[:, P * h:P * (h + 1)], ATT[:, t, h, :], GV[:, 512 * t + P * h:512 * t + P * (h + 1)], h == 0, False, True)
            for c in range(4):
                t, r = c // 2, slice(64 * (c % 2), 64 * (c % 2) + 64)
                if c:
                    pe.wait_ge(sg_ok, c)
                    for h in range(2):
                        ins = mm(bank(2 + t)[r, 256 * h:256 * (h + 1)], QB[:, h, L * c:L * (c + 1)], SG[:, 256 * h:256 * (h + 1)],
                                 False, c == 3, True)
                    ins.then_inc(go_used if c < 3 else go_ps, 1)
                if c < 3:
                    for h in range(2):
                        ins = mm(bank(7)[:, 256 * h:256 * (h + 1)], KLT[r, t, h, :], GV[r, 512 * t + 256 * h:512 * t + 256 * (h + 1)])
                    ins.then_inc(sg_ps, 1)
            for t in range(TT):
                ins = mm(bank(5 + t), L2[:, P * t:P * (t + 1)], G2[:, :])
            ins.then_inc(gate_ps, 1)

            pe.wait_ge(y_rw, 1)
            pe.wait_ge(y_gla, 1)
            transposes(YT, 0)
            pe.wait_ge(wout_in, 16)
            pe.wait_ge(ut_a, 8)
            pe.wait_ge(ut_v, 8)
            wo = slot(4, 4).rearrange("p (k n) -> p k n", k=KC)
            for k in range(KC):
                for t in range(TT):
                    for half in range(2):
                        ins = mm(bank(4 + 2 * t + half), UT3[:, k, P * t:P * (t + 1)], wo[:, k, 512 * half:512 * (half + 1)],
                                 k == 0, k == KC - 1, True)
                        if k == KC - 1 and t == 0 and half == 1:
                            ins.then_inc(wout_ps, 1)
            ins.then_inc(wout_used, 1)
            pe.wait_ge(brow_in, 32)
            pe.wait_ge(scaled, 2)
            for i in range(16):
                ins = pe.transpose(bank(5)[:, NE * i:NE * (i + 1)], B1R[0:NE, P * i:P * (i + 1)], ID[0:NE, 0:NE])
            ins.then_inc(b1_ps, 1)
            pe.wait_ge(u2_ok, 2)
            transposes(U2, 0)
            pe.wait_ge(ut_a, 12)
            pe.wait_ge(ut_v, 12)
            for t in range(TT):
                o = bank(6)[:, NE * t:NE * (t + 1)]
                mm(o, ONES[0:1, :], BR[0:1, :], True, False)
                for k in range(KC):
                    ins = mm(o, UT3[:, k, P * t:P * (t + 1)], WR3[:, k, :], False, k == KC - 1)
            ins.then_inc(lg_ps, 1)
            pe.wait_ge(sel_ok, 1)
            ms = RT8[3]
            mm(bank(7)[:, 0:NE], SU[:, :], ms[:, 0, 0:NE])
            mm(bank(7)[:, NE:2 * NE], ONES[:, :], ms[:, 0, 0:NE], True, False)
            mm(bank(7)[:, NE:2 * NE], SU[:, :], ms[:, 1, 0:NE], False, True)
            mm(bank(7)[:, 2 * NE:3 * NE], ONES[:, :], ms[:, 0, 0:NE], True, False)
            mm(bank(7)[:, 2 * NE:3 * NE], ONES[:, :], ms[:, 1, 0:NE], False, True).then_inc(pos_ps, 1)
            pe.wait_ge(gates_ok, 1)
            for t in range(TT):
                ins = pe.transpose(bank(6)[0:NE, P * t:P * (t + 1)], GAT3[:, t, 0:NE], ID[:, :])
            ins.then_inc(gtt_ps, 1)
            pe.wait_ge(gt_ok, 1)
            for t in range(TT):
                for half in range(2):
                    mm(bank(2 * t + half), GT[0:NE, P * t:P * (t + 1)], B2R[0:NE, 512 * half:512 * (half + 1)], True, False, True)

            def gather():
                for k in range(KC):
                    for t in range(TT):
                        ins = mm(bank(6)[:, SLOTS * k:SLOTS * (k + 1)], U2[:, t, P * k:P * (k + 1)], OH3[:, t, :],
                                 k == 0 and t == 0, t == 1, True)
                ins.then_inc(gathered, 1)

            def scatter(done, last=False):
                for t in range(TT):
                    for half in range(2):
                        r = slice(64 * half, 64 * half + 64)
                        ins = mm(bank(2 * t + half), OHGT[r, P * t:P * (t + 1)], YS[r, :], False, last, True)
                ins.then_inc(done, 1)

            pe.wait_ge(oh_ok, 1)
            gather()
            pe.wait_ge(cnt_ok, 1)
            pe.wait_ge(b1_ok, 1)

            def item(i, e):
                pe.wait_ge(xg_ok, i + 1)
                pe.wait_ge(t_ok, i * 2 + 1)
                pe.wait_ge(landed[KC - 1], e * 16 + 16)
                for k in range(KC):
                    pe.wait_ge(landed[k], e * 16 + 16)
                    w = slot(k)
                    for half in range(2):
                        mm(bank(4 + half)[0:64, :], XG[:, k, :], w[:, 512 * half:512 * (half + 1)], k == 0, k == KC - 1, True)
                        ins = mm(bank(4 + half)[64:128, :], XG[:, k, :], w[:, FF + 512 * half:FF + 512 * (half + 1)], k == 0, k == KC - 1, True)
                        if k == KC - 1 and half == 0:
                            ins.then_inc(h0_ps, 1)
                    ins.then_inc(w1_used, 1)
                pe.wait_ge(ys_ok, i + 1)
                scatter(scattered)
                pe.wait_ge(ohg_ok, i + 1)
                for t in range(TT):
                    ins = pe.transpose(bank(7)[:, P * t:P * (t + 1)], OHG3[:, t, :], ID[:, :])
                ins.then_inc(ohgt_ps, 1)
                pe.wait_ge(hs0, i + 1)
                for c in range(KC):
                    if c == 4:
                        pe.wait_ge(hs1, i + 1)
                    ins = pe.transpose(bank(4 + c // 4)[:, P * (c % 4):P * (c % 4 + 1)], HS[:, P * c:P * (c + 1)], ID[:, :])
                    if c % 4 == 3:
                        ins.then_inc(t_ps, 1)
                pe.wait_ge(oh_ok, i + 2)
                gather()
                pe.wait_ge(ohgt_ok, i + 1)
                for k in range(KC):
                    if k % 4 == 0:
                        pe.wait_ge(act_ok, i * 2 + (k // 4 + 1))
                    if k % 2 == 0:
                        pe.wait_ge(landed[8 + k // 2], e * 16 + 16)
                    w = slot(8 + k // 2)[:, 1024 * (k % 2):1024 * (k % 2 + 1)]
                    mm(bank(7)[0:64, :], ACTT[:, k, :], w[:, 0:512], k == 0, k == KC - 1, True)
                    ins = mm(bank(7)[64:128, :], ACTT[:, k, :], w[:, 512:1024], k == 0, k == KC - 1, True)
                    if k % 2:
                        ins.then_inc(w2_used, 1)

            def experts(nb):
                with pe.Fori(0, NE) as e:
                    for b in range(nb):
                        item(e * nb + b, e)
                pe.wait_ge(ys_ok, NE * nb + 1)
                scatter(acc_done, True)

            most = pe.value_load(CNTI[0:1, 0:1], min_val=0, max_val=T)
            with pe.If(most > SLOTS):
                experts(NBMAX)
            with pe.Else():
                experts(1)

            pe.wait_ge(ple_in, 48)
            for k in range(2):
                for t in range(TT):
                    ins = pe.transpose(bank(4)[:, 256 * k + P * t:256 * k + P * (t + 1)], PX[:, t, P * k:P * (k + 1)], ID[:, :])
            ins.then_inc(pt_ps, 1)
            pe.wait_ge(pt_ok, 1)
            pe.wait_ge(u2_ok, 4)
            transposes(U2, 4)
            pe.wait_ge(ut_a, 16)
            pe.wait_ge(ut_v, 16)
            for t in range(TT):
                for half in range(2):
                    for k in range(KC):
                        ins = mm(bank(2 * t + half), UT3[:, k, P * t:P * (t + 1)], PLG[:, k, 512 * half:512 * (half + 1)], k == 0, k == KC - 1)
            ins.then_inc(pg_ps, 1)
            for t in range(TT):
                for half in range(2):
                    for k in range(2):
                        ins = mm(bank(4 + 2 * t + half), PT[:, k, P * t:P * (t + 1)], PLW[:, k, 512 * half:512 * (half + 1)], k == 0, k == 1)
            ins.then_inc(pw_ps, 1)


_INS = ["x", "p", "norm_mix", "w_in", "shift_mu", "rw_w0", "rw_w2", "rw_a0", "rw_a2", "rw_g2", "rw_kk", "rw_ka", "rw_rk",
        "rw_gn_w", "rw_gn_b", "gla_gk2", "gla_gk_b", "gla_norm", "w_out", "norm_ffn", "w_router", "b_router",
        "w1", "b1", "w2", "b2", "norm_ple", "w_ple_gate", "w_ple", "norm_final"]


def kernel(**inputs):
    import numpy as _np
    import concourse.bacc as _bacc
    from concourse import mybir as _mybir
    from concourse.bass_utils import run_bass_kernel_spmd as _run

    nc = _bacc.Bacc("TRN2", target_bir_lowering=False, num_devices=1)
    arrays, args = {}, []
    for name in _INS:
        a = _np.ascontiguousarray(inputs[name])
        arrays[f"in_{name}_dram"] = a
        args.append(nc.dram_tensor(f"in_{name}_dram", a.shape, _mybir.dt.from_np(a.dtype), kind="ExternalInput").ap())
    args.append(nc.dram_tensor("out_0_dram", (1, T, D), F32, kind="ExternalOutput").ap())
    hybrid_block(nc, *args)
    r = _run(nc, [arrays], core_ids=[0])
    return r.results[0]["out_0_dram"]
```

```python
from contextlib import ExitStack
from math import exp

import concourse.bass as bass
from concourse import mybir

F32 = mybir.dt.float32
I32 = mybir.dt.int32
ALU = mybir.AluOpType
ACT = mybir.ActivationFunctionType
AX = mybir.AxisListType

P = 128
T = 256
TT = T // P
D = 1024
KC = D // P
L = 64
NCH = T // L
RW = 512
HP = 4
NH = 8
RWC = 3 * RW + 256
GH = 4
GQ = 256
GV_W = 512
NE = 32
FF = 1024
SLOTS = 64
NBMAX = T // SLOTS
SLOT_F = 2048
NSLOT = 12
XSLOT = 7
BANK = 512
NEG = -1.0e30
EPS = 1e-6
GN_EPS = 64e-5
DECAY = exp(-0.5)
TEMP = 16.0
LEADS = ((0, 5, 7), (5, 10, 4), (10, NE // 2 - 1, 0))
START = 2
GO = (5, 7)
TOK_ORDER = (0, 1, 4, 5, 6, 7, 2, 3)

VROWS = [("norm_mix", 8), ("norm_ffn", 8), ("norm_ple", 8), ("shift_mu", 14), ("rw_w0", 4), ("rw_a0", 4),
         ("rw_kk", 4), ("rw_ka", 4), ("rw_rk", 4), ("gla_gk_b", 2)]
VAT = {}
_n = 0
for _name, _k in VROWS:
    VAT[_name] = _n
    _n += _k
NV = _n


def hybrid_block(nc, x, p, norm_mix, w_in, shift_mu, rw_w0, rw_w2, rw_a0, rw_a2, rw_g2, rw_kk, rw_ka, rw_rk,
                 rw_gn_w, rw_gn_b, gla_gk2, gla_gk_b, gla_norm, w_out, norm_ffn, w_router, b_router,
                 w1, b1, w2, b2, norm_ple, w_ple_gate, w_ple, norm_final, out):
    vec_src = {
        "norm_mix": norm_mix.rearrange("a (n q) -> (a n) q", q=P), "norm_ffn": norm_ffn.rearrange("a (n q) -> (a n) q", q=P),
        "norm_ple": norm_ple.rearrange("a (n q) -> (a n) q", q=P), "shift_mu": shift_mu.rearrange("a (n q) -> (a n) q", q=P),
        "rw_w0": rw_w0.rearrange("a (n q) -> (a n) q", q=P), "rw_a0": rw_a0.rearrange("a (n q) -> (a n) q", q=P),
        "rw_kk": rw_kk.rearrange("a (n q) -> (a n) q", q=P), "rw_ka": rw_ka.rearrange("a (n q) -> (a n) q", q=P),
        "rw_rk": rw_rk.rearrange("a (n h) q -> (a n) (h q)", h=2), "gla_gk_b": gla_gk_b.rearrange("a (n q) -> (a n) q", q=P),
    }
    with ExitStack() as ctx:
        def sem(name):
            return ctx.enter_context(nc.semaphore(name))

        RING = ctx.enter_context(nc.sbuf_tensor("ring", [P, NSLOT * SLOT_F], F32))
        PS = ctx.enter_context(nc.psum_tensor("ps", [P, 8 * BANK], F32))

        def sb(name, n, dt=F32):
            return ctx.enter_context(nc.sbuf_tensor(name, [P, n], dt))

        def slot(i, n=1):
            return RING[:, i * SLOT_F:(i + n) * SLOT_F]

        def bank(b, n=1):
            return PS[:, b * BANK:(b + n) * BANK]

        XB = sb("xb", 2048)
        UT = sb("ut", 2048)
        T34 = sb("t34", 2048)
        KRR = sb("krr", 2048)
        AR = sb("ar", 2048)
        BK = sb("bk", 2048)
        AY = sb("ay", 2048)
        BKV = sb("bkv", 4096)
        GVG = sb("gvg", 2048)
        GQK = sb("gqk", 1024)
        LWB = sb("lwb", 2304)
        VEC = sb("vec", P)
        VC = sb("vc", 64)
        OMU = sb("omu", 16)
        OMKA = sb("omka", 4)
        LW, G2, MK, LB = LWB[:, 0:512], LWB[:, 512:1024], LWB[:, 1024:1536], LWB[:, 1536:2304]
        DL, GK2, DGW = BKV[:, 3072:3712], BKV[:, 3712:3968], BKV[:, 3968:4096]
        WR = sb("wr", KC * NE)
        BR = sb("br", NE)
        SL = sb("sl", P)
        SU = sb("su", P)
        D1L = sb("d1l", P)
        D1U = sb("d1u", P)
        BD = sb("bd", P)
        BDG = sb("bdg", 256)
        ID = sb("id", P)
        ONES = sb("ones", P)
        RM = sb("rm", T)
        IOTA = sb("iota", P)
        PLC = sb("plc", 16)
        EM = sb("em", 24)
        BON = sb("bon", 16)
        SM = sb("sm", 128)
        SM2 = sb("sm2", 64)
        POSB = sb("posb", NBMAX * TT * (NE + 1))
        GATES = sb("gates", TT * (NE + 1))
        RT = sb("rt", 8 * 72)
        OH = sb("oh", TT * SLOTS)
        OHG = sb("ohg", TT * P)
        OHGT = sb("ohgt", T)
        CMAX = sb("cmax", 1)
        CNTI = sb("cnti", 1, I32)

        T1, T2 = XB[:, 0:1024], XB[:, 1024:2048]
        T3, T4 = T34[:, 0:1024], T34[:, 1024:2048]
        KR, RR = KRR[:, 0:1024], KRR[:, 1024:2048]
        BF, KF = BK[:, 0:1024], BK[:, 1024:2048]
        Bt, Kt, Vt = BKV[:, 0:1024], BKV[:, 1024:2048], BKV[:, 2048:3072]
        GV, GG = GVG[:, 0:1024], GVG[:, 1024:2048]
        L1, L2, DGK = LB[:, 0:256], LB[:, 256:512], LB[:, 512:768]
        XB3 = XB[:, :].rearrange("p (t d) -> p t d", t=TT)
        UT3 = UT[:, :].rearrange("p (k t) -> p k t", k=KC)
        AR5 = AR[:, :].rearrange("p (h t w c) -> p h t w c", h=HP, t=TT, w=2)
        AY4 = AY[:, :].rearrange("p (t h w) -> p t h w", t=TT, h=NH)
        WR3 = WR[:, :].rearrange("p (k e) -> p k e", k=KC)

        def hp3(a):
            return a.rearrange("p (h t) -> p h t", h=HP)

        MT = slot(0, 4).rearrange("p (m w) -> p m w", m=16)
        TAB = slot(4).rearrange("p (m w) -> p m w", m=16)
        X_ = slot(5).rearrange("p (m w) -> p m w", m=16)
        XT_ = slot(6).rearrange("p (m w) -> p m w", m=16)
        Y_ = slot(7).rearrange("p (m w) -> p m w", m=16)
        QE, KE, QB, KL = (slot(8)[:, 512 * i:512 * (i + 1)].rearrange("p (h t) -> p h t", h=2) for i in range(4))
        ATT = slot(9)[:, 0:1024].rearrange("p (t h w) -> p t h w", t=TT, h=GH)
        KLT = slot(9)[:, 1024:1536].rearrange("p (t h w) -> p t h w", t=TT, h=2)
        SG = slot(9)[:, 1536:2048]
        GLT = [slot(7)[:, 512 * i:512 * (i + 1)] for i in range(4)]
        WU = slot(10).rearrange("p (w t h d) -> p w t h d", w=2, t=TT, h=NH)
        WM, U0 = (slot(10)[:, 1024 * i:1024 * (i + 1)].rearrange("p (t c) -> p t c", t=TT) for i in range(2))
        REFF = slot(11)[:, 0:1024].rearrange("p (t h w) -> p t h w", t=TT, h=HP)
        GTS = slot(11)[:, 1024:2048].rearrange("p (c h w) -> p c h w", c=2, h=HP)
        HS_ = T34[:, 0:1536].rearrange("p (c w) -> p c w", c=3)
        SRW = BK[:, 0:1536].rearrange("p (c h w) -> p c h w", c=3, h=HP)
        ROWS = UT[:, 0:1536].rearrange("p (r w) -> p r w", r=3)
        YT = AR[:, :].rearrange("p (t d) -> p t d", t=TT)
        HS = T34[:, 0:1024]
        TP = T34[:, 1024:2048].rearrange("p (c w) -> p c w", c=KC)
        XG = GQK[:, 0:512].rearrange("p (k s) -> p k s", k=KC)
        GLU, LIN, SIG, ACTT = (AY[:, 512 * i:512 * (i + 1)].rearrange("p (k s) -> p k s", k=KC) for i in range(4))
        YS = GVG[:, 0:512]
        B1T = GVG[:, 512:512 + NE * 16].rearrange("p (e c g) -> p e c g", e=NE, g=2)
        GATE = GQK
        GTMP = KRR[:, 1024:2048]
        GSIG = KRR[:, 0:1024]
        B1R = BKV[:, 0:2048]
        OH3 = OH[:, :].rearrange("p (t s) -> p t s", t=TT)
        OHG3 = OHG[:, :].rearrange("p (t s) -> p t s", t=TT)
        POS4 = POSB[:, :].rearrange("p (b t e) -> p b t e", b=NBMAX, t=TT)
        GAT3 = GATES[:, :].rearrange("p (t e) -> p t e", t=TT)
        RT8 = [RT[:, 72 * i:72 * (i + 1)].rearrange("p (t e) -> p t e", t=TT) for i in range(8)]
        XTRA = (BK[:, :], LWB[:, 0:2048], KRR[:, :], AR[:, :], UT[:, :], BKV[:, 0:2048], BKV[:, 2048:4096])
        PLG = slot(0, 4).rearrange("p (k n) -> p k n", k=KC)
        PLW = slot(4).rearrange("p (k n) -> p k n", k=2)
        PX = slot(5)[:, 0:512].rearrange("p (t n) -> p t n", t=TT)
        PT = slot(5)[:, 512:1024].rearrange("p (k t) -> p k t", k=2)
        NF = slot(5)[:, 1024:2048]
        RES = slot(6).rearrange("p (t d) -> p t d", t=TT)
        ZG = AR[:, :]

        def col(name, i, n=1):
            return VC[:, VAT[name] + i:VAT[name] + i + n]

        x_in, vec_in, small_in, wout_in, brow_in, out_done = (
            sem(s) for s in ("x_in", "vec_in", "small_in", "wout_in", "brow_in", "out_done"))
        win = [sem(f"win{i}") for i in range(8)]
        landed = [sem(f"landed{i}") for i in range(NSLOT)]
        landed_x = win[0:XSLOT]
        ple_in = sem("ple_in")
        masks, id_ok = sem("masks"), sem("id_ok")
        vec_t, vc_ok = sem("vec_t"), sem("vc_ok")
        rstd_sq, scaled = sem("rstd_sq"), sem("scaled")
        xt_ps, ut_v, ut_a = sem("xt_ps"), sem("ut_v"), sem("ut_a")
        tile_ps, tile_a, tile_v, tile_g = sem("tile_ps"), sem("tile_a"), sem("tile_v"), sem("tile_g")
        lora_act, z_ps, a_ps, sz_ok, iclr_ok = sem("lora_act"), sem("z_ps"), sem("a_ps"), sem("sz_ok"), sem("iclr_ok")
        sq_ok, ss_ps, ss_max, nrm_ok = sem("sq_ok"), sem("ss_ps"), sem("ss_max"), sem("nrm_ok")
        gv_ps, gg_ps, gk_ps, gvg_ok = sem("gv_ps"), sem("gg_ps"), sem("gk_ps"), sem("gvg_ok")
        cs_ok, exp_ok, exp_used = sem("cs_ok"), sem("exp_ok"), sem("exp_used")
        kf_ok, a_ok, r_ok, rkk_ok = sem("kf_ok"), sem("a_ok"), sem("r_ok"), sem("rkk_ok")
        tok_ps, tok_a, tok_v, bon_ps, bon_ok = sem("tok_ps"), sem("tok_a"), sem("tok_v"), sem("bon_ps"), sem("bon_ok")
        mat_ps, mat_ok, x1_ok, x1t_ok = sem("mat_ps"), sem("mat_ok"), sem("x1_ok"), sem("x1t_ok")
        y_ps, y_ok, xx_ps, xx_ok = sem("y_ps"), sem("y_ok"), sem("xx_ps"), sem("xx_ok")
        mv_ps, mv_ok, wu_ps, wu_ok = sem("mv_ps"), sem("mv_ok"), sem("wu_ps"), sem("wu_ok")
        reff_ps, reff_ok, h_ps, gt_ps, st_ok, st_ps = (
            sem("reff_ps"), sem("reff_ok"), sem("h_ps"), sem("gt_ps"), sem("st_ok"), sem("st_ps"))
        o_ps, gate_ps, osq_v, osq_a, ovar, orstd, y_rw = (
            sem("o_ps"), sem("gate_ps"), sem("osq_v"), sem("osq_a"), sem("ovar"), sem("orstd"), sem("y_rw"))
        gx_ok, gln_ok, gla_la, gb_ok, gdiff, gexp, gla_el = (
            sem("gx_ok"), sem("gln_ok"), sem("gla_la"), sem("gb_ok"), sem("gdiff"), sem("gexp"), sem("gla_el"))
        klt_ps, klt_ok, att_ps, att_ok, sg_ps, sg_ok, go_ps, gsig, ggn = (
            sem("klt_ps"), sem("klt_ok"), sem("att_ps"), sem("att_ok"), sem("sg_ps"), sem("sg_ok"), sem("go_ps"), sem("gsig"), sem("ggn"))
        y_gla, bv_ok = sem("y_gla"), sem("bv_ok")
        wout_ps, wout_used, lg_ps, lg_max, lg_exp, sel_ok, pos_ps, cnt_ok, gt_ok, gtt_ps, gates_ok = (
            sem("wout_ps"), sem("wout_used"), sem("lg_ps"), sem("lg_max"), sem("lg_exp"), sem("sel_ok"), sem("pos_ps"), sem("cnt_ok"),
            sem("gt_ok"), sem("gtt_ps"), sem("gates_ok"))
        b1_ps, b1_ok = sem("b1_ps"), sem("b1_ok")
        oh_ok, ohg_ok, gathered, xg_ok = sem("oh_ok"), sem("ohg_ok"), sem("gathered"), sem("xg_ok")
        h0_ps, w1_used, hs0, hs1 = sem("h0_ps"), sem("w1_used"), sem("hs0"), sem("hs1")
        scattered, ohgt_ps, ohgt_ok, t_ps, t_ok = sem("scattered"), sem("ohgt_ps"), sem("ohgt_ok"), sem("t_ps"), sem("t_ok")
        glu_ok, sig_ok, act_ok, w2_used, ys_ok = sem("glu_ok"), sem("sig_ok"), sem("act_ok"), sem("w2_used"), sem("ys_ok")
        acc_done, pt_ps, pt_ok, pg_ps, pw_ps, psig = (
            sem("acc_done"), sem("pt_ps"), sem("pt_ok"), sem("pg_ps"), sem("pw_ps"), sem("psig"))
        fin = sem("fin")
        vch, ach, gch = sem("vch"), sem("ach"), sem("gch")
        xs_ok, go_used, lin_ok, gl_ok, gk_read = (
            sem("xs_ok"), sem("go_used"), sem("lin_ok"), sem("gl_ok"), sem("gk_read"))
        gate_ok, rs_ok, zero_ps = sem("gate_ok"), sem("rs_ok"), sem("zero_ps")

        def linker(eng, chain):
            count = {}

            def signal(ins, s=None):
                s = s or chain
                count[id(s)] = count.get(id(s), 0) + 1
                ins.then_inc(s, 1)
                return s

            def settle(s=None):
                s = s or chain
                eng.wait_ge(s, count[id(s)])

            def link(ins, s=None):
                settle(signal(ins, s))

            return signal, settle, link

        def transposed_at(n, k):
            return KC * n + ((k // 2 * 2 + 4) % KC if n == 1 else k // 2 * 2) + 2

        w1_v = w1.rearrange("a e (k q) n -> a e q k n", q=P)
        w2_v = w2.rearrange("a e (k q) n -> a e q k n", q=P)

        block = ctx.enter_context(nc.Block())

        @block.sync
        def _(sp):
            sp.dma_start(XB3, x.rearrange("a (t q) d -> q (a t) d", q=P)).then_inc(x_in, 16)
            for name, k in VROWS:
                sp.dma_start(VEC[VAT[name]:VAT[name] + k, :], vec_src[name]).then_inc(vec_in, 16)

            def load_cols(i, s, n, c0, w):
                dst = RING[:, s * SLOT_F:s * SLOT_F + KC * w].rearrange("p (k n) -> p k n", k=KC)
                sp.dma_start(dst, w_in[0, :, c0:c0 + w].rearrange("(k q) n -> q k n", q=P)).then_inc(win[i], 16)

            def load_w1(e, k):
                sp.dma_start(slot(k), w1_v[0, e, :, k, :]).then_inc(landed[k], 16)

            def load_w2(e, j):
                sp.dma_start(slot(8 + j).rearrange("p (k n) -> p k n", k=2), w2_v[0, e, :, 2 * j:2 * j + 2, :]
                             ).then_inc(landed[8 + j], 16)

            def load_extra(e, k):
                sp.dma_start(XTRA[k], w1_v[0, e, :, k, :]).then_inc(landed_x[k], 16)

            load_cols(0, 0, 1, 3 * RW, 256)
            sp.dma_start(LW[0:64, :], rw_w2[0]).then_inc(small_in, 16)
            sp.dma_start(LW[64:128, :], rw_a2[0]).then_inc(small_in, 16)
            sp.dma_start(G2[:, :], rw_g2[0]).then_inc(small_in, 16)
            sp.dma_start(GK2[0:16, :], gla_gk2[0]).then_inc(small_in, 16)
            sp.dma_start(DGW[:, :].rearrange("p (k n) -> p k n", k=KC),
                         w_in[0, :, RWC + 2 * GQ + 2 * GV_W:].rearrange("(k q) n -> q k n", q=P)).then_inc(small_in, 16)
            sp.dma_start(WR3, w_router[0].rearrange("(k q) e -> q k e", q=P)).then_inc(small_in, 16)
            sp.dma_start(BR[:, :], b_router.partition_broadcast(P)).then_inc(small_in, 16)
            load_cols(1, 1, 2, RW, 512)
            load_cols(2, 3, 2, 0, 512)
            load_cols(3, 5, 2, 2 * RW, 512)
            load_cols(4, 7, 2, RWC, 512)
            load_cols(5, 9, 2, RWC + 2 * GQ, 512)
            load_cols(6, 11, 1, RWC + 2 * GQ + GV_W, 256)
            sp.wait_ge(tile_ps, 2)
            load_cols(7, 0, 1, RWC + 2 * GQ + GV_W + 256, 256)
            sp.wait_ge(gg_ps, 2)
            for r, src in enumerate((rw_gn_w, rw_gn_b, gla_norm)):
                sp.dma_start(ROWS[:, r, :], src[0].partition_broadcast(P)).then_inc(small_in, 16)
            sp.wait_ge(rkk_ok, 1)
            sp.wait_ge(bon_ps, 1)
            sp.wait_ge(r_ok, 1)
            sp.dma_start(XB3, x.rearrange("a (t q) d -> q (a t) d", q=P)).then_inc(x_in, 16)
            sp.wait_ge(att_ok, 2)
            sp.wait_ge(gate_ok, 2)
            load_extra(1, 1)
            sp.wait_ge(wu_ok, 4)
            sp.dma_start(slot(4, 4).rearrange("p (k n) -> p k n", k=KC),
                         w_out[0].rearrange("(k q) n -> q k n", q=P)).then_inc(wout_in, 16)

            sp.wait_ge(go_ps, 1)
            for j in range(2):
                load_w2(0, j)
            sp.wait_ge(reff_ps, 1)
            for k in range(2):
                load_w1(0, k)
            sp.wait_ge(h_ps, 3)
            for k in range(2, 4):
                load_w1(0, k)
            sp.wait_ge(o_ps, 1)
            sp.wait_ge(bv_ok, 1)
            sp.dma_start(B1R[0:NE, :], b1[0]).then_inc(brow_in, 16)
            for j in range(2, 4):
                load_w2(0, j)
            load_extra(1, 0)
            load_extra(1, 6)
            sp.wait_ge(y_rw, 1)
            load_extra(1, 2)
            sp.wait_ge(ys_ok, 1)
            for half in range(2):
                sp.dma_start(YS[64 * half:64 * half + NE, :], b2[0, :, 512 * half:512 * (half + 1)]).then_inc(brow_in, 16)
            sp.wait_ge(xt_ps, 2 * KC)
            load_extra(1, 3)
            sp.wait_ge(wout_used, 1)
            for k in range(4, 8):
                load_w1(0, k)
            sp.wait_ge(lg_ps, 1)
            load_extra(1, 4)
            sp.wait_ge(b1_ps, 1)
            load_extra(1, 5)

            def stream(nb):
                two = 2 * nb

                def even_done(h, k):
                    sp.wait_ge(w1_used, h * (two * KC) + ((nb - 1) * KC + k + 1))

                def odd_done(h, k):
                    sp.wait_ge(w1_used, h * (two * KC) + ((two - 1) * KC + k + 1))

                def w2_done(h, j, odd):
                    sp.wait_ge(w2_used, h * (two * 4) + (((odd + 1) * nb - 1) * 4 + j + 1))

                def next_even(h, ks):
                    for k in ks:
                        even_done(h, k)
                        load_w1(h * 2 + 2, k)

                def next_odd(h, ks):
                    for k in ks:
                        odd_done(h, k)
                        load_extra(h * 2 + 3, k)

                def rest(h, odd):
                    for k in range(XSLOT, KC):
                        (odd_done if odd else even_done)(h, k)
                        load_w1(h * 2 + (odd + 1), k)
                    for j in range(4):
                        w2_done(h, j, odd)
                        load_w2(h * 2 + (odd + 1), j)

                for first, last, ahead in LEADS:
                    with sp.Fori(first, last) as h:
                        next_even(h, range(ahead))
                        rest(h, 0)
                        next_even(h, range(ahead, XSLOT))
                        next_odd(h, range(ahead))
                        rest(h, 1)
                        next_odd(h, range(ahead, XSLOT))
                rest(NE // 2 - 1, 0)
                even_done(NE // 2 - 1, KC - 2)

            sp.wait_ge(cnt_ok, 1)
            most = sp.value_load(CNTI[0:1, 0:1], min_val=0, max_val=T)
            with sp.If(most > SLOTS):
                stream(NBMAX)
            with sp.Else():
                stream(1)
            sp.dma_start(PX, p.rearrange("a b (t q) n -> q (a b t) n", q=P)).then_inc(ple_in, 16)
            sp.dma_start(PLW, w_ple[0].rearrange("(k q) n -> q k n", q=P)).then_inc(ple_in, 16)
            sp.dma_start(PLG, w_ple_gate[0].rearrange("(k q) n -> q k n", q=P)).then_inc(wout_in, 16)
            sp.dma_start(NF, norm_final.partition_broadcast(P)).then_inc(brow_in, 16)
            for t in range(TT):
                sp.wait_ge(fin, t + 1)
                sp.dma_start(out[0, P * t:P * (t + 1), :], RES[:, t, :]).then_inc(out_done, 16)
            sp.wait_ge(out_done, 32)

        @block.gpsimd
        def _(pool):
            signal, settle, link = linker(pool, gch)
            ones = T34[:, 0:P]
            bds = [T34[:, P * (i + 1):P * (i + 2)] for i in range(7)]

            def block_diagonal(dst, s, width):
                v = dst.rearrange("p (b c) -> p b c", c=width)
                nb = v.shape[1]
                link(pool.memset(dst, 1.0))
                link(pool.affine_select(out=v, in_=v, compare_op=ALU.is_ge, fill=0.0, base=0,
                                        pattern=[[-s, nb], [0, width]], channel_multiplier=1))
                link(pool.affine_select(out=v, in_=v, compare_op=ALU.is_ge, fill=0.0, base=s - 1,
                                        pattern=[[s, nb], [0, width]], channel_multiplier=-1))

            link(pool.memset(ones, 1.0))
            block_diagonal(bds[0], 1, 1)
            pool.tensor_copy(ID[:, :], bds[0]).then_inc(id_ok, 1)
            pool.wait_ge(id_ok, 1)
            for i in range(1, 7):
                block_diagonal(bds[i], 1 << i, 1 << i)
            block_diagonal(BDG[:, :], 64, 128)
            signal(pool.tensor_copy(BD[:, :], bds[6]))
            signal(pool.memset(ONES[:, :], 1.0))
            signal(pool.memset(RM[:, :], 1.0))
            link(pool.affine_select(out=SU[:, :], in_=ones, compare_op=ALU.is_gt, fill=0.0, base=0,
                                    pattern=[[1, P]], channel_multiplier=-1))
            link(pool.affine_select(out=SL[:, :], in_=ones, compare_op=ALU.is_gt, fill=0.0, base=0,
                                    pattern=[[-1, P]], channel_multiplier=1))
            link(pool.memset(RM[:, :].rearrange("p (c t) -> p c t", c=NCH)[:, :, 0:1], 0.0))
            link(pool.tensor_tensor(SL[:, :], SL[:, :], BD[:, :], ALU.mult))
            link(pool.tensor_tensor(MK[:, 0:P], SU[:, :], BD[:, :], ALU.mult))
            link(pool.tensor_tensor(MK[:, P:2 * P], MK[:, 0:P], ID[:, :], ALU.add))
            link(pool.tensor_copy(MK[:, 2 * P:4 * P], MK[:, 0:2 * P]))
            link(pool.tensor_tensor(D1L[:, :], bds[1], bds[0], ALU.subtract))
            link(pool.tensor_tensor(D1U[:, :], D1L[:, :], SU[:, :], ALU.mult))
            link(pool.tensor_tensor(D1L[:, :], D1L[:, :], SL[:, :], ALU.mult))
            for i in range(5):
                d = DL[:, P * i:P * (i + 1)]
                link(pool.tensor_tensor(d, bds[i + 2], bds[i + 1], ALU.subtract))
                link(pool.tensor_tensor(d, d, SL[:, :], ALU.mult))
            link(pool.iota(IOTA[:, :], pattern=[[0, 2], [1, SLOTS]], base=0, channel_multiplier=0,
                           allow_small_or_imprecise_dtypes=True))
            pool.memset(POSB[:, :], -5.0).then_inc(masks, 1)
            pool.wait_ge(masks, 1)
            pool.memset(OHGT[:, :], 0.0).then_inc(masks, 1)
            pool.wait_ge(masks, 2)
            pool.memset(RT[:, :], NEG).then_inc(masks, 1)
            pool.wait_ge(masks, 3)
            pool.memset(GATES[:, :], 0.0).then_inc(masks, 1)
            pool.wait_ge(masks, 4)
            pool.memset(OHG[:, :], 0.0).then_inc(masks, 1)

            xg, ab, la, bs = GLT
            pool.wait_ge(gx_ok, 1)
            link(pool.tensor_scalar(xg, xg, 0.0, None, ALU.min))
            pool.wait_ge(gln_ok, 1)
            link(pool.tensor_tensor(la, xg, ab, ALU.subtract), gla_la)
            pool.wait_ge(gb_ok, 1)
            b4 = bs.rearrange("p (h c t) -> p h c t", h=2, c=NCH)
            d4 = la.rearrange("p (h c t) -> p h c t", h=2, c=NCH)
            mid, last = b4[:, :, :, L // 2 - 1:L // 2], b4[:, :, :, L - 1:L]
            for h in range(2):
                signal(pool.tensor_tensor(d4[:, h], b4[:, h], mid[:, h].broadcast_to([P, NCH, L]), ALU.subtract))
            em3 = EM[:, :].rearrange("p (w h c) -> p w h c", w=3, h=2)
            signal(pool.tensor_copy(em3[:, 0], mid.rearrange("p h c o -> p h (c o)")))
            signal(pool.tensor_tensor(em3[:, 1], last.rearrange("p h c o -> p h (c o)"), mid.rearrange("p h c o -> p h (c o)"), ALU.subtract))
            signal(pool.tensor_copy(em3[:, 2], last.rearrange("p h c o -> p h (c o)")))
            settle()
            pool.memset(SM[:, 120:121], 0.0).then_inc(gdiff, 1)
            pool.wait_ge(gdiff, 1)
            pool.wait_ge(gexp, 3)
            g4 = GQK[:, :].rearrange("p (h t) -> p h t", h=4)
            ep, en = xg.rearrange("p (h t) -> p h t", h=2), ab.rearrange("p (h t) -> p h t", h=2)
            link(pool.tensor_scalar(ep, ep, float(GQ // GH) ** -0.5, None, ALU.mult))
            signal(pool.tensor_tensor(QE, g4[:, 0:2], ep, ALU.mult))
            link(pool.tensor_tensor(KE, g4[:, 2:4], en, ALU.mult))
            for h in range(2):
                def c3(a):
                    return a[:, h].rearrange("p (c t) -> p c t", c=NCH)
                signal(pool.tensor_tensor(c3(QB), c3(QE), em3[:, 0, h].unsqueeze(2).broadcast_to([P, NCH, L]), ALU.mult))
                signal(pool.tensor_tensor(c3(KL), c3(KE), em3[:, 1, h].unsqueeze(2).broadcast_to([P, NCH, L]), ALU.mult))
            settle()
            pool.memset(SM[:, 121:122], 0.0).then_inc(gla_el, 1)
            pool.wait_ge(gla_el, 1)
            for u in range(8):
                m2 = slice(2 * u, 2 * u + 2)
                pool.wait_ge(mat_ok, u + 1)
                link(pool.tensor_tensor(X_[:, m2, :], TAB[:, m2, :], D1L[:, :].unsqueeze(1).broadcast_to([P, 2, P]), ALU.mult))
                signal(pool.tensor_tensor(X_[:, m2, :], X_[:, m2, :], ID[:, :].unsqueeze(1).broadcast_to([P, 2, P]), ALU.add), x1_ok)
                signal(pool.tensor_tensor(XT_[:, m2, :], XT_[:, m2, :], ID[:, :].unsqueeze(1).broadcast_to([P, 2, P]), ALU.add), x1t_ok)
            pool.wait_ge(small_in, 16 * 10)
            pool.wait_ge(gsig, 1)
            gg3 = GG.rearrange("p (t w) -> p t w", t=TT)
            link(pool.tensor_tensor(GG, GG, GSIG, ALU.mult))
            pool.tensor_tensor(gg3, gg3, ROWS[:, 2:3, :].broadcast_to([P, TT, 512]), ALU.mult).then_inc(ggn, 1)
            pool.wait_ge(bon_ok, 1)
            pool.wait_ge(tok_v, 4)
            pool.wait_ge(tok_a, 4)
            pool.tensor_tensor(GTMP.rearrange("p (g d) -> p g d", d=L), Vt.rearrange("p (g d) -> p g d", d=L),
                               BON[:, :].unsqueeze(2).broadcast_to([P, 16, L]), ALU.mult).then_inc(bv_ok, 1)

        @block.scalar
        def _(act):
            signal, settle, link = linker(act, ach)

            def square_sums(n, src, junk):
                for t in range(TT):
                    link(act.activation(junk, src[:, t, :], ACT.Square, accum_out=SM[:, 4 * n + t:4 * n + t + 1]))
                act.activation(SM[:, 4 * n + 2:4 * n + 4], SM[:, 4 * n:4 * n + 2], ACT.Sqrt, bias=EPS, scale=1.0 / D
                               ).then_inc(rstd_sq, 1)

            act.wait_ge(x_in, 16)
            square_sums(0, XB3, T34[:, 1024:2048])
            act.wait_ge(vec_t, 1)
            act.activation(VC[:, 0:NV], bank(7)[:, 0:NV], ACT.Copy).then_inc(vc_ok, 1)
            act.wait_ge(vc_ok, 1)
            link(act.activation(OMU[:, 0:14], col("shift_mu", 0, 14), ACT.Copy, scale=-1.0, bias=1.0))
            link(act.activation(OMKA[:, 0:4], col("rw_ka", 0, 4), ACT.Copy, scale=-1.0, bias=1.0), vc_ok)

            def transposed(n, gain, ks=(0, 1, 4, 5)):
                for k in ks:
                    act.wait_ge(xt_ps, transposed_at(n, k))
                    src = PS[:, 256 * k:256 * (k + 1)]
                    if gain:
                        act.activation(UT3[:, k, :], src, ACT.Copy, scale=col(gain, k)).then_inc(ut_a, 1)
                    else:
                        act.activation(UT3[:, k, :], src, ACT.Copy).then_inc(ut_a, 1)

            transposed(0, "norm_mix")

            tile_dst = [L1, L2] + [KR[:, 256 * i:256 * (i + 1)] for i in range(4)] + [RR[:, 256 * i:256 * (i + 1)] for i in range(4)] \
                + [T4[:, 256 * i:256 * (i + 1)] for i in range(4)]
            mu_at = [12, 13] + [4, 5, 6, 7] + [0, 1, 2, 3] + [8, 9, 10, 11]

            def shift_half(n):
                act.wait_ge(tile_ps, n + 1)
                if n == 10:
                    act.wait_ge(masks, 1)
                act.activation(tile_dst[n], PS[:, (4 + n % 4) * BANK:(4 + n % 4) * BANK + T], ACT.Copy,
                               scale=OMU[:, mu_at[n]:mu_at[n] + 1]).then_inc(tile_a, 1)

            for n in range(2):
                shift_half(n)
            act.wait_ge(tile_v, 2)
            signal(act.activation(L1[0:64, :], L1[0:64, :], ACT.Tanh), lora_act)
            signal(act.activation(L2, L2, ACT.Sigmoid), lora_act)
            for n in range(2, 6):
                shift_half(n)
            act.wait_ge(z_ps, 1)
            act.wait_ge(xt_ps, KC)
            for h in range(HP):
                act.activation(T1[:, 256 * h:256 * (h + 1)], PS[:, 256 * h:256 * (h + 1)], ACT.Sigmoid,
                               bias=col("rw_w0", h)).then_inc(sz_ok, 1)
            act.wait_ge(a_ps, 1)
            for h in range(HP):
                act.activation(T2[:, 256 * h:256 * (h + 1)], PS[:, 1024 + 256 * h:1024 + 256 * (h + 1)], ACT.Sigmoid,
                               bias=col("rw_a0", h)).then_inc(iclr_ok, 1)
            for n in range(6, 14):
                shift_half(n)
            act.wait_ge(ss_max, 1)
            act.activation(BF, BF, ACT.Sqrt).then_inc(nrm_ok, 1)

            def tile_g_out(i):
                n = 14 + i
                act.wait_ge(tile_ps, n + 1)
                dst = GQK[:, 256 * i:256 * (i + 1)] if i < 4 else DGK[0:16, :]
                m = P if i < 4 else 16
                act.activation(dst, PS[0:m, (4 + n % 4) * BANK:(4 + n % 4) * BANK + T], ACT.Copy).then_inc(tile_g, 1)

            act.wait_ge(cs_ok, 1)
            act.activation(AR5[:, :, :, 0, :], T1.rearrange("p (h t c) -> p h t c", h=HP, t=TT), ACT.Exp, scale=-DECAY).then_inc(exp_ok, 1)
            tile_g_out(0)
            act.wait_ge(exp_used, 1)
            act.activation(T1, T3, ACT.Exp, scale=DECAY).then_inc(exp_ok, 1)
            tile_g_out(1)
            act.wait_ge(exp_used, 2)
            act.activation(T1, T3, ACT.Exp, scale=-DECAY).then_inc(exp_ok, 1)
            for i in range(2, 5):
                tile_g_out(i)
            act.wait_ge(gv_ps, 1)
            signal(act.activation(GV[:, 0:512], bank(2), ACT.Copy), gvg_ok)
            xg, ab, la, bs = GLT
            act.wait_ge(gk_ps, 1)
            act.wait_ge(tile_ps, 18)
            for h in range(2):
                src = bank(7)[:, 256 * h:256 * (h + 1)]
                signal(act.activation(xg[:, 256 * h:256 * (h + 1)], src, ACT.Identity, bias=col("gla_gk_b", h)))
            for h in range(2):
                src = bank(7)[:, 256 * h:256 * (h + 1)]
                signal(act.activation(ab[:, 256 * h:256 * (h + 1)], src, ACT.Abs, bias=col("gla_gk_b", h)), gk_read)
            settle()
            act.wait_ge(gk_read, 2)
            act.activation(ab, ab, ACT.Exp, scale=-1.0).then_inc(gx_ok, 1)
            act.wait_ge(gx_ok, 1)
            act.activation(ab, ab, ACT.Ln, bias=1.0).then_inc(gln_ok, 1)
            act.wait_ge(gv_ps, 2)
            signal(act.activation(GV[:, 512:1024], bank(3), ACT.Copy), gvg_ok)
            for i, (grp, dst) in enumerate(((0, Vt), (1, Vt), (4, Bt), (5, Bt))):
                act.wait_ge(tok_ps, TOK_ORDER.index(grp) + 1)
                act.activation(dst[:, 512 * (i % 2):512 * (i % 2 + 1)], bank(grp), ACT.Copy).then_inc(tok_a, 1)
            act.wait_ge(gdiff, 1)
            act.activation(xg, la, ACT.Exp, scale=1.0 / TEMP).then_inc(gexp, 1)
            act.activation(ab, la, ACT.Exp, scale=-1.0 / TEMP).then_inc(gexp, 1)
            act.activation(EM[:, :], EM[:, :], ACT.Exp, scale=1.0 / TEMP).then_inc(gexp, 1)
            for t in range(TT):
                act.wait_ge(gg_ps, t + 1)
                signal(act.activation(GG[:, 512 * t:512 * (t + 1)], bank(0 + t), ACT.Copy), gvg_ok)
            act.wait_ge(klt_ps, 1)
            act.activation(KLT, bank(4).rearrange("p (t h w) -> p t h w", t=TT, h=2), ACT.Copy).then_inc(klt_ok, 1)
            for t in range(TT):
                act.wait_ge(gate_ps, t + 1)
                act.activation(GATE[:, 512 * t:512 * (t + 1)], bank(4 if t else 7), ACT.Copy).then_inc(gate_ok, 1)
            act.wait_ge(gvg_ok, 4)
            act.wait_ge(mat_ok, 8)
            act.activation(GSIG, GG, ACT.Sigmoid).then_inc(gsig, 1)
            for g in range(4):
                act.wait_ge(mv_ps, g + 1)
                act.activation(AY4[:, g // 2, 4 * (g % 2):4 * (g % 2) + 4, 64:128],
                               bank(2 * g)[:, 0:256].rearrange("p (h w) -> p h w", h=4), ACT.Copy).then_inc(mv_ok, 1)
            act.wait_ge(go_ps, 1)
            act.wait_ge(ggn, 1)
            for t in range(TT):
                signal(act.activation(KRR[:, 512 * t:512 * (t + 1)], bank(GO[t]), ACT.Square), osq_a)
            act.wait_ge(ovar, 1)
            act.activation(SM[:, 48:56], SM[:, 40:48], ACT.Sqrt, bias=EPS, scale=1.0 / 128).then_inc(orstd, 1)
            transposed(1, None, (4, 5))
            act.wait_ge(osq_v, 1)
            act.activation(T34[:, 0:1024], KRR[:, 0:1024], ACT.Square).then_inc(osq_a, 1)
            act.wait_ge(ovar, 2)
            act.activation(SM2[:, 32:48], SM2[:, 16:32], ACT.Sqrt, bias=GN_EPS, scale=1.0 / L).then_inc(orstd, 1)
            transposed(1, None, (6, 7, 0, 1))
            for t in range(TT):
                act.wait_ge(scaled, t + 1)
                link(act.activation(T34[:, 1024:2048], XB3[:, t, :], ACT.Square, accum_out=SM[:, 8 + t:9 + t]))
            act.activation(SM[:, 10:12], SM[:, 8:10], ACT.Sqrt, bias=EPS, scale=1.0 / D).then_inc(rstd_sq, 1)
            transposed(2, "norm_ffn")
            act.wait_ge(lg_max, 1)
            for t in range(TT):
                act.activation(RT8[1][:, t, 0:NE], RT8[0][:, t, 0:NE], ACT.Exp, bias=SM[:, 100 + t:101 + t]).then_inc(lg_exp, 1)
            act.wait_ge(gtt_ps, 1)
            act.wait_ge(zero_ps, 2)
            act.activation(OHGT[:, :], bank(7)[:, 0:T], ACT.Copy).then_inc(gt_ok, 1)
            act.wait_ge(cnt_ok, 1)

            def item(i):
                act.wait_ge(h0_ps, i + 1)
                act.activation(HS[:, 0:512], bank(4), ACT.Copy).then_inc(hs0, 1)
                act.wait_ge(ohgt_ps, i + 1)
                act.wait_ge(scattered, i + 1)
                act.activation(OHGT[:, :], bank(7)[:, 0:T], ACT.Copy).then_inc(ohgt_ok, 1)
                for g in range(2):
                    act.wait_ge(glu_ok, i * 2 + (g + 1))
                    act.activation(SIG[:, 4 * g:4 * g + 4], GLU[:, 4 * g:4 * g + 4], ACT.Sigmoid, scale=1.702).then_inc(sig_ok, 1)
                act.wait_ge(w2_used, i * 4 + 4)
                act.activation(YS, bank(7), ACT.Copy).then_inc(ys_ok, 1)

            def experts(nb):
                with act.Fori(0, NE) as e:
                    for b in range(nb):
                        item(e * nb + b)

            most = act.value_load(CNTI[0:1, 0:1], min_val=0, max_val=T)
            with act.If(most > SLOTS):
                experts(NBMAX)
            with act.Else():
                experts(1)
            act.wait_ge(pt_ps, 1)
            act.activation(PT, bank(4).rearrange("p (k t) -> p k t", k=2), ACT.Copy).then_inc(pt_ok, 1)
            for t in range(TT):
                act.wait_ge(scaled, 3 + t)
                link(act.activation(T34[:, 1024:2048], XB3[:, t, :], ACT.Square, accum_out=SM[:, 12 + t:13 + t]))
            act.activation(SM[:, 14:16], SM[:, 12:14], ACT.Sqrt, bias=EPS, scale=1.0 / D).then_inc(rstd_sq, 1)
            transposed(3, "norm_ple")
            act.wait_ge(rs_ok, 2)
            for i in range(4):
                t = i // 2
                act.wait_ge(pg_ps, i + 1)
                act.activation(ZG[:, 512 * i:512 * (i + 1)], bank(i), ACT.Sigmoid, scale=SM[:, 26 + t:27 + t]).then_inc(psig, 1)
                if i == 2:
                    act.wait_ge(scaled, 6)
                    link(act.activation(T34[:, 1024:2048], XB3[:, 0, :], ACT.Square, accum_out=SM[:, 16:17]))
                    act.activation(SM[:, 18:19], SM[:, 16:17], ACT.Sqrt, bias=EPS, scale=1.0 / D).then_inc(rstd_sq, 1)
            act.wait_ge(scaled, 8)
            link(act.activation(T34[:, 1024:2048], XB3[:, 1, :], ACT.Square, accum_out=SM[:, 17:18]))
            act.activation(SM[:, 19:20], SM[:, 17:18], ACT.Sqrt, bias=EPS, scale=1.0 / D).then_inc(rstd_sq, 1)

        @block.vector
        def _(dve):
            signal, settle, link = linker(dve, vch)

            def transposed(n, gain, ks=(2, 3, 6, 7)):
                for k in ks:
                    dve.wait_ge(xt_ps, transposed_at(n, k))
                    src = PS[:, 256 * k:256 * (k + 1)]
                    if gain:
                        dve.tensor_scalar(UT3[:, k, :], src, col(gain, k), None, ALU.mult).then_inc(ut_v, 1)
                    else:
                        dve.tensor_copy(UT3[:, k, :], src).then_inc(ut_v, 1)

            dve.wait_ge(x_in, 16)
            dve.wait_ge(rstd_sq, 1)
            link(dve.reciprocal(SM[:, 20:22], SM[:, 2:4]))
            for t in range(TT):
                dve.tensor_scalar(XB3[:, t, :], XB3[:, t, :], SM[:, 20 + t:21 + t], None, ALU.mult).then_inc(xs_ok, 1)
            dve.wait_ge(vc_ok, 1)
            transposed(0, "norm_mix")

            tile_dst = [L1, L2] + [KR[:, 256 * i:256 * (i + 1)] for i in range(4)] + [RR[:, 256 * i:256 * (i + 1)] for i in range(4)] \
                + [T4[:, 256 * i:256 * (i + 1)] for i in range(4)]
            mu_at = [12, 13] + [4, 5, 6, 7] + [0, 1, 2, 3] + [8, 9, 10, 11]

            def shift(n):
                dve.wait_ge(tile_a, n + 1)
                src = PS[:, (4 + n % 4) * BANK:(4 + n % 4) * BANK + T - 1]
                d = tile_dst[n][:, 1:T]
                dve.scalar_tensor_tensor(out=d, in0=src, scalar=col("shift_mu", mu_at[n]), in1=d, op0=ALU.mult,
                                         op1=ALU.add).then_inc(tile_v, 1)

            for n in range(6):
                shift(n)
            dve.wait_ge(tile_v, 6)
            for h in range(HP):
                signal(dve.tensor_scalar(hp3(KF)[:, h], hp3(KR)[:, h], col("rw_kk", h), None, ALU.mult))
            settle()
            link(dve.tensor_tensor(BF, KF, KF, ALU.mult), sq_ok)
            for n in range(6, 10):
                shift(n)
            dve.wait_ge(iclr_ok, 4)
            dve.wait_ge(masks, 1)
            for h in range(HP):
                signal(dve.tensor_scalar(hp3(T3)[:, h], hp3(T2)[:, h], col("rw_ka", h), OMKA[:, h:h + 1], ALU.mult, ALU.add))
            settle()
            link(dve.tensor_tensor(KR, KR, T3, ALU.mult))
            dve.wait_ge(sz_ok, 4)
            dve.wait_ge(masks, 1)
            for h in range(HP):
                signal(dve.tensor_tensor_scan(out=hp3(T3)[:, h], data0=RM[:, :], data1=hp3(T1)[:, h], initial=0.0,
                                              op0=ALU.mult, op1=ALU.add))
            settle()
            for n in range(10, 14):
                shift(n)
            link(dve.tensor_tensor(T1, T3, T1, ALU.subtract), cs_ok)
            dve.wait_ge(ss_ps, 1)
            link(dve.tensor_scalar(BF, bank(0, 2), 1e-24, None, ALU.max), ss_max)
            dve.wait_ge(nrm_ok, 1)
            link(dve.reciprocal(BF, BF))
            link(dve.tensor_tensor(KF, KF, BF, ALU.mult))
            dve.wait_ge(exp_ok, 1)
            kf4 = KF.rearrange("p (h t c) -> p h t c", h=HP, t=TT)
            for h in range(HP):
                signal(dve.scalar_tensor_tensor(out=AR5[:, h, :, 0, :], in0=AR5[:, h, :, 0, :], scalar=-1.0, in1=kf4[:, h],
                                                op0=ALU.mult, op1=ALU.mult), a_ok)
            signal(dve.tensor_tensor(BF, KF, T2, ALU.mult), exp_used)
            settle(exp_used)
            settle(a_ok)
            dve.wait_ge(exp_ok, 2)
            signal(dve.tensor_tensor(KF, KR, T1, ALU.mult), kf_ok)
            link(dve.tensor_tensor(BF, BF, T1, ALU.mult), exp_used)
            dve.wait_ge(exp_ok, 3)
            r4, t4 = RR.rearrange("p (h t c) -> p h t c", h=HP, t=TT), T1.rearrange("p (h t c) -> p h t c", h=HP, t=TT)
            signal(dve.tensor_copy(PLC[:, :], T1.rearrange("p (g c) -> p g c", c=L)[:, :, L - 1]))
            for h in range(HP):
                signal(dve.tensor_tensor(AR5[:, h, :, 1, :], r4[:, h], t4[:, h], ALU.mult))
            link(dve.tensor_tensor(T2, RR, KR, ALU.mult), r_ok)
            for h in range(HP):
                signal(dve.tensor_scalar(hp3(T2)[:, h], hp3(T2)[:, h], col("rw_rk", h), None, ALU.mult))
            settle()
            dve.memset(SM[:, 122:123], 0.0).then_inc(rkk_ok, 1)
            for i, grp in enumerate((6, 7)):
                dve.wait_ge(tok_ps, TOK_ORDER.index(grp) + 1)
                dve.tensor_copy(AY4[:, i, :, 0:64], bank(grp).rearrange("p (h w) -> p h w", h=NH)).then_inc(tok_v, 1)
            for i, grp in enumerate((2, 3)):
                dve.wait_ge(tok_ps, TOK_ORDER.index(grp) + 1)
                dve.tensor_copy(Kt[:, 512 * i:512 * (i + 1)], bank(grp)).then_inc(tok_v, 1)
            dve.wait_ge(gla_la, 1)
            for q in range(2):
                signal(dve.tensor_tensor_scan(out=GLT[3][:, 256 * q:256 * (q + 1)], data0=RM[:, :],
                                              data1=GLT[2][:, 256 * q:256 * (q + 1)], initial=0.0,
                                              op0=ALU.mult, op1=ALU.add))
            settle()
            dve.memset(SM[:, 124:125], 0.0).then_inc(gb_ok, 1)
            dve.wait_ge(bon_ps, 1)
            dve.tensor_copy(BON[:, :], bank(2)[:, 0:16]).then_inc(bon_ok, 1)
            dve.wait_ge(gg_ps, 2)
            dve.wait_ge(masks, 1)
            mk1 = MK[:, :]
            for u in range(8):
                t, h = u // 4, u % 4
                b0 = 4 * ((u + 1) % 2)
                dve.wait_ge(mat_ps, u + 1)
                for j in range(2):
                    m = 8 * t + 2 * h + j
                    signal(dve.tensor_tensor(MT[:, m, :], bank(b0 + j), mk1, ALU.mult))
                    signal(dve.tensor_tensor(TAB[:, m, :], bank(b0 + 2 + j)[:, 0:P], SL[:, :], ALU.mult))
                settle()
                m2 = slice(8 * t + 2 * h, 8 * t + 2 * h + 2)
                dve.tensor_tensor(XT_[:, m2, :], MT[:, m2, 0:P], D1U[:, :].unsqueeze(1).broadcast_to([P, 2, P]), ALU.mult).then_inc(mat_ok, 1)
            dve.wait_ge(x1_ok, 8)
            dve.wait_ge(x1t_ok, 8)
            dve.wait_ge(att_ps, 1)
            for j in range(2):
                signal(dve.tensor_tensor(ATT[:, :, j:GH:2, :], bank(5 + j).rearrange("p (t h w) -> p t h w", t=TT, h=2),
                                         MK[:, P:2 * P].unsqueeze(1).unsqueeze(1).broadcast_to([P, TT, 2, P]), ALU.mult), att_ok)
            dve.wait_ge(gla_el, 1)
            sgt = T34[:, 0:512]
            em3 = EM[:, :].rearrange("p (w h c) -> p w h c", w=3, h=2)

            def gla_state(c):
                dve.wait_ge(sg_ps, c + 1)
                dst = SG if c == 0 else sgt
                if c:
                    dve.wait_ge(go_used, c)
                s2 = SG.rearrange("p (h w) -> p h w", h=2)
                ins = dve.tensor_tensor(dst.rearrange("p (h w) -> p h w", h=2), bank(3).rearrange("p (h w) -> p h w", h=2),
                                        BDG[:, :].unsqueeze(1).broadcast_to([P, 2, 256]), ALU.mult)
                if c == 0:
                    link(ins, sg_ok)
                else:
                    signal(ins)
                    link(dve.tensor_tensor(s2, s2, em3[:, 2, :, c:c + 1].broadcast_to([P, 2, 256]), ALU.mult))
                    link(dve.tensor_tensor(SG, SG, sgt, ALU.add), sg_ok)

            for lv in range(5):
                for g in range(4):
                    dve.wait_ge(y_ps, 4 * lv + g + 1)
                    link(dve.tensor_tensor(Y_[:, 4 * g:4 * g + 4, :], bank(2 * g).rearrange("p (m w) -> p m w", m=4),
                                           DL[:, P * lv:P * (lv + 1)].unsqueeze(1).broadcast_to([P, 4, P]), ALU.mult), y_ok)
                if lv == 4:
                    gla_state(0)
                for g in range(4):
                    if lv == 4 and g == 2:
                        gla_state(1)
                    dve.wait_ge(xx_ps, 4 * lv + g + 1)
                    if lv < 4:
                        signal(dve.tensor_tensor(X_[:, 4 * g:4 * g + 4, :], bank(2 * g + 1).rearrange("p (m w) -> p m w", m=4),
                                                 X_[:, 4 * g:4 * g + 4, :], ALU.add), xx_ok)
                    link(dve.tensor_tensor(XT_[:, 4 * g:4 * g + 4, :], bank(2 * g).rearrange("p (m w) -> p m w", m=4),
                                           XT_[:, 4 * g:4 * g + 4, :], ALU.add), xx_ok)
            for g in range(4):
                dve.wait_ge(wu_ps, g + 1)
                dve.tensor_copy(WU[:, :, g // 2, 4 * (g % 2):4 * (g % 2) + 4, :].rearrange("p w h d -> p h w d"),
                                bank(2 * g).rearrange("p (h w d) -> p h w d", h=4, w=2)).then_inc(wu_ok, 1)
            hb = (2, 4, 3)
            gb = (6, 6)
            rb = (3, 2)
            stb = (4, 2)
            bdb = BD[:, :].unsqueeze(1).broadcast_to([P, HP, P])

            def h4(a):
                return a.rearrange("p (h w) -> p h w", h=HP)

            def added(c):
                dve.wait_ge(h_ps, c + 1)
                signal(dve.tensor_tensor(h4(HS_[:, c]), h4(bank(hb[c])), bdb, ALU.mult))

            def transition(c):
                dve.wait_ge(gt_ps, c)
                signal(dve.tensor_tensor(GTS[:, c - 1], h4(bank(gb[c - 1])), bdb, ALU.mult))

            def pl(c):
                return PLC[:, :].rearrange("p (h c) -> p h c", h=HP)[:, :, c:c + 1].broadcast_to([P, HP, P])

            def state(c):
                dve.wait_ge(st_ps, c)
                link(dve.tensor_tensor(HS_[:, c], bank(stb[c - 1]), HS_[:, c], ALU.add))
                link(dve.tensor_tensor(SRW[:, c], h4(HS_[:, c]), pl(c), ALU.mult), st_ok)

            gla_state(2)
            added(0)
            transition(1)
            settle()
            link(dve.tensor_tensor(SRW[:, 0], h4(HS_[:, 0]), pl(0), ALU.mult))
            added(1)
            settle()
            dve.memset(SM[:, 127:128], 0.0).then_inc(st_ok, 1)
            for t in range(TT):
                dve.wait_ge(reff_ps, t + 1)
                dve.tensor_tensor(REFF[:, t], bank(rb[t]).rearrange("p (h w) -> p h w", h=HP), AR5[:, :, t, 1, :], ALU.add).then_inc(reff_ok, 1)
            transition(2)
            state(1)
            dve.wait_ge(osq_a, 2)
            link(dve.tensor_reduce(SM[:, 40:48], KRR[:, 0:1024].rearrange("p (g w) -> p g w", g=8), AX.X, ALU.add), ovar)
            dve.wait_ge(orstd, 1)
            link(dve.reciprocal(SM[:, 56:64], SM[:, 48:56]))
            dve.wait_ge(ggn, 1)
            yg = YT[:, :, 512:1024]
            for t in range(TT):
                signal(dve.tensor_tensor(yg[:, t].rearrange("p (h w) -> p h w", h=GH), bank(GO[t]).rearrange("p (h w) -> p h w", h=GH),
                                         SM[:, 56 + 4 * t:60 + 4 * t].unsqueeze(2).broadcast_to([P, GH, P]), ALU.mult))
            settle()
            link(dve.tensor_tensor(yg, yg, GG.rearrange("p (t w) -> p t w", t=TT), ALU.mult), y_gla)
            added(2)
            settle()
            state(2)
            oc = KRR[:, 0:1024]
            og = oc.rearrange("p (g d) -> p g d", d=L)
            ob = bank(0, 2).rearrange("p (g d) -> p g d", d=L)
            dve.wait_ge(o_ps, 1)
            link(dve.tensor_reduce(SM2[:, 0:16], ob, AX.X, ALU.add))
            link(dve.tensor_scalar(SM2[:, 0:16], SM2[:, 0:16], 1.0 / L, None, ALU.mult))
            link(dve.tensor_tensor(og, ob, SM2[:, 0:16].unsqueeze(2).broadcast_to([P, 16, L]), ALU.subtract), osq_v)
            dve.wait_ge(osq_a, 3)
            link(dve.tensor_reduce(SM2[:, 16:32], T34[:, 0:1024].rearrange("p (g d) -> p g d", d=L), AX.X, ALU.add), ovar)
            dve.wait_ge(orstd, 2)
            link(dve.reciprocal(SM2[:, 48:64], SM2[:, 32:48]))
            link(dve.tensor_tensor(og, og, SM2[:, 48:64].unsqueeze(2).broadcast_to([P, 16, L]), ALU.mult))
            o3 = oc.rearrange("p (t w) -> p t w", t=TT)
            dve.wait_ge(small_in, 16 * 10)
            link(dve.tensor_tensor(o3, o3, ROWS[:, 0:1, :].broadcast_to([P, TT, 512]), ALU.mult))
            link(dve.tensor_tensor(o3, o3, ROWS[:, 1:2, :].broadcast_to([P, TT, 512]), ALU.add))
            dve.wait_ge(bv_ok, 1)
            link(dve.tensor_tensor(oc, oc, GTMP, ALU.add))
            dve.wait_ge(gate_ok, 2)
            link(dve.tensor_tensor(YT[:, :, 0:512], GATE[:, :].rearrange("p (t w) -> p t w", t=TT), o3, ALU.mult), y_rw)
            transposed(1, None, (2, 3))
            dve.wait_ge(go_ps, 1)
            dve.memset(YS, 0.0).then_inc(ys_ok, 1)
            dve.wait_ge(x_in, 32)
            for t in range(TT):
                dve.wait_ge(wout_used if t else wout_ps, 1)
                signal(dve.tensor_tensor(XB3[:, t, :], bank(4 + 2 * t, 2), XB3[:, t, :], ALU.add), scaled)
            transposed(2, "norm_ffn")
            dve.wait_ge(rstd_sq, 2)
            link(dve.reciprocal(SM[:, 24:26], SM[:, 10:12]), rs_ok)
            dve.wait_ge(masks, 5)
            dve.wait_ge(lg_ps, 1)
            lg, ex, mr, ms, top = RT8[0], RT8[1], RT8[2], RT8[3], RT8[4]
            for t in range(TT):
                signal(dve.scalar_tensor_tensor(out=lg[:, t, 0:NE], in0=bank(6)[:, NE * t:NE * (t + 1)], scalar=SM[:, 24 + t:25 + t],
                                                in1=BR[:, :], op0=ALU.mult, op1=ALU.add))
            settle()
            for t in range(TT):
                signal(dve.max(top[:, t, 0:8], lg[:, t, 0:NE + 4]))
            settle()
            link(dve.tensor_scalar(SM[:, 100:102], top[:, :, 0:1].rearrange("p t o -> p (t o)"), -1.0, None, ALU.mult), lg_max)
            link(dve.memset(top[:, :, 4:8], NEG))
            for t in range(TT):
                signal(dve.match_replace(mr[:, t, 0:NE + 4], top[:, t, 0:8], lg[:, t, 0:NE + 4], 2 * NEG))
            settle()
            signal(dve.tensor_tensor(ms[:, :, 0:NE], mr[:, :, 0:NE], lg[:, :, 0:NE], ALU.not_equal), sel_ok)
            settle(sel_ok)
            dve.wait_ge(lg_exp, 2)
            link(dve.tensor_tensor(ex[:, :, 0:NE], ex[:, :, 0:NE], ms[:, :, 0:NE], ALU.mult))
            link(dve.tensor_reduce(SM[:, 104:106], ex[:, :, 0:NE], AX.X, ALU.add))
            link(dve.reciprocal(SM[:, 106:108], SM[:, 104:106]))
            gain = SM[:, 106:108].unsqueeze(2).broadcast_to([P, TT, NE])
            signal(dve.tensor_tensor(GAT3[:, :, 0:NE], ex[:, :, 0:NE], gain, ALU.mult))
            for c in (0, 64):
                signal(dve.tensor_tensor(OHG3[:, :, c:c + NE], ex[:, :, 0:NE], gain, ALU.mult), gates_ok)
            settle(gates_ok)
            settle()
            dve.wait_ge(pos_ps, 1)
            pp = RT8[5]
            link(dve.scalar_tensor_tensor(out=pp[:, :, 0:NE], in0=bank(7)[:, 0:TT * NE].rearrange("p (t e) -> p t e", t=TT),
                                          scalar=1.0, in1=ms[:, :, 0:NE], op0=ALU.add, op1=ALU.mult))
            for b in range(NBMAX):
                signal(dve.tensor_scalar(POS4[:, b, :, 0:NE], pp[:, :, 0:NE], -1.0 - SLOTS * b, None, ALU.add))
            signal(dve.tensor_reduce(CMAX[:, :], bank(7)[:, 64:96], AX.X, ALU.max))
            settle()
            link(dve.tensor_copy(CNTI[:, :], CMAX[:, :]), cnt_ok)

            def one_hot(b, e):
                for t in range(TT):
                    ins = dve.tensor_scalar(OH3[:, t, :], IOTA[:, 0:SLOTS], POS4[:, b, t, bass.ds(e, 1)],
                                            SM[:, 24 + t:25 + t], ALU.is_equal, ALU.mult)
                    if t == TT - 1:
                        ins.then_inc(oh_ok, 1)

            def gather_evac():
                dve.tensor_tensor(XG, bank(6).rearrange("p (k s) -> p k s", k=KC),
                                  col("norm_ffn", 0, 8).unsqueeze(2).broadcast_to([P, KC, SLOTS]), ALU.mult).then_inc(xg_ok, 1)

            one_hot(0, 0)
            dve.wait_ge(b1_ps, 1)
            dve.wait_ge(gvg_ok, 4)
            link(dve.tensor_copy(B1T.rearrange("p e c g -> p g c e"), bank(5).rearrange("p (g c e) -> p g c e", g=2, c=8)), b1_ok)
            dve.wait_ge(gtt_ps, 1)
            dve.wait_ge(gathered, 1)
            gather_evac()

            def item(i, b, e, nb_, ne_):
                for t in range(TT):
                    ins = dve.tensor_scalar(OHG3[:, t, :], IOTA[:, :], POS4[:, b, t, bass.ds(e, 1)], GAT3[:, t, bass.ds(e, 1)],
                                            ALU.is_equal, ALU.mult)
                    if t == TT - 1:
                        ins.then_inc(ohg_ok, 1)
                one_hot(nb_, ne_)
                dve.wait_ge(w1_used, i * KC + KC)
                dve.tensor_copy(HS[:, 512:1024], bank(5)).then_inc(hs1, 1)
                for g in range(2):
                    cs = slice(4 * g, 4 * g + 4)
                    dve.wait_ge(t_ps, i * 2 + (g + 1))
                    dve.tensor_tensor(TP[:, cs].rearrange("p c (g s) -> p c g s", g=2),
                                      bank(4 + g).rearrange("p (c g s) -> p c g s", c=4, g=2),
                                      B1T[:, bass.ds(e, 1), cs, :].rearrange("p e c g -> p (e c) g").unsqueeze(3).broadcast_to([P, 4, 2, SLOTS]),
                                      ALU.add).then_inc(t_ok, 1)
                    dve.wait_ge(t_ok, i * 2 + (g + 2))
                    dve.tensor_scalar(GLU[:, cs], TP[:, cs, 0:SLOTS], 7.0, None, ALU.min).then_inc(glu_ok, 1)
                    dve.tensor_scalar(LIN[:, cs], TP[:, cs, SLOTS:P], 7.0, -7.0, ALU.min, ALU.max).then_inc(lin_ok, 1)
                    dve.wait_ge(glu_ok, i * 2 + (g + 1))
                    dve.wait_ge(lin_ok, i * 2 + (g + 1))
                    dve.scalar_tensor_tensor(out=LIN[:, cs], in0=LIN[:, cs], scalar=1.0, in1=GLU[:, cs], op0=ALU.add,
                                             op1=ALU.mult).then_inc(gl_ok, 1)
                for g in range(2):
                    cs = slice(4 * g, 4 * g + 4)
                    dve.wait_ge(gl_ok, i * 2 + (g + 1))
                    dve.wait_ge(sig_ok, i * 2 + (g + 1))
                    dve.tensor_tensor(ACTT[:, cs], LIN[:, cs], SIG[:, cs], ALU.mult).then_inc(act_ok, 1)
                dve.wait_ge(gathered, i + 2)
                gather_evac()

            def experts(nb):
                with dve.Fori(0, NE) as e:
                    for b in range(nb):
                        item(e * nb + b, b, e, (b + 1) % nb, e + (b + 1) // nb)

            dve.memset(SM[:, 125:126], 0.0).then_inc(t_ok, 1)
            most = dve.value_load(CNTI[0:1, 0:1], min_val=0, max_val=T)
            with dve.If(most > SLOTS):
                experts(NBMAX)
            with dve.Else():
                experts(1)
            dve.wait_ge(acc_done, 1)
            for t in range(TT):
                signal(dve.tensor_tensor(XB3[:, t, :], bank(2 * t, 2), XB3[:, t, :], ALU.add), scaled)
            transposed(3, "norm_ple")
            dve.wait_ge(rstd_sq, 3)
            link(dve.reciprocal(SM[:, 26:28], SM[:, 14:16]), rs_ok)
            dve.wait_ge(pw_ps, 1)
            dve.wait_ge(brow_in, 64)
            settle(scaled)

            def final(t):
                dve.wait_ge(rstd_sq, 4 + t)
                link(dve.reciprocal(SM[:, 28 + t:29 + t], SM[:, 18 + t:19 + t]))
                dve.scalar_tensor_tensor(out=RES[:, t, :], in0=XB3[:, t, :], scalar=SM[:, 28 + t:29 + t], in1=NF,
                                         op0=ALU.mult, op1=ALU.mult).then_inc(fin, 1)

            for i in range(4):
                t, half = i // 2, i % 2
                dve.wait_ge(psig, i + 1)
                zg, xb = ZG[:, 512 * i:512 * (i + 1)], XB3[:, t, 512 * half:512 * (half + 1)]
                link(dve.tensor_tensor(zg, bank(4 + i), zg, ALU.mult))
                signal(dve.tensor_tensor(xb, xb, zg, ALU.add), scaled)
                if i == 2:
                    final(0)
            final(1)

        @block.tensor
        def _(pe):
            def mm(out_, lhs, rhs, start=True, stop=True, shared=False):
                return pe.matmul(out_, lhs, rhs, start=start, stop=stop, skip_group_check=shared)

            pe.wait_ge(id_ok, 1)
            pe.wait_ge(vec_in, 16 * len(VROWS))
            pe.transpose(bank(7)[:, 0:NV], VEC[0:NV, :], ID[0:NV, 0:NV]).then_inc(vec_t, 1)

            def transposes(src, ks=range(KC)):
                for k in ks:
                    for t in range(TT):
                        ins = pe.transpose(PS[:, 256 * k + P * t:256 * k + P * (t + 1)],
                                           src[:, t, P * k:P * (k + 1)], ID[:, :])
                    ins.then_inc(xt_ps, 1)

            pe.wait_ge(xs_ok, 2)
            transposes(XB3)

            def tile(n, w):
                if n >= 4:
                    if n - 4 < 14:
                        pe.wait_ge(tile_v, n - 3)
                    else:
                        pe.wait_ge(tile_g, n - 4 - 13)
                m = w(0).shape[1]
                for k in range(KC):
                    ins = mm(PS[0:m, (4 + n % 4) * BANK:(4 + n % 4) * BANK + T], w(k), UT3[:, k, :], k == 0, k == KC - 1)
                ins.then_inc(tile_ps, 1)

            def cols(s, w):
                return RING[:, s * SLOT_F:s * SLOT_F + KC * w].rearrange("p (k n) -> p k n", k=KC)

            pe.wait_ge(ut_v, 4)
            pe.wait_ge(ut_a, 4)
            pe.wait_ge(vc_ok, 2)
            pe.wait_ge(win[0], 16)
            for i in range(2):
                tile(i, lambda k: cols(0, 256)[:, k, P * i:P * (i + 1)])
            pe.wait_ge(win[1], 16)
            for i in range(4):
                tile(2 + i, lambda k: cols(1, 512)[:, k, P * i:P * (i + 1)])
            pe.wait_ge(small_in, 16 * 7)
            pe.wait_ge(lora_act, 2)
            for h in range(HP):
                ins = mm(PS[:, 256 * h:256 * (h + 1)], LW[0:64, P * h:P * (h + 1)], L1[0:64, :])
            ins.then_inc(z_ps, 1)
            for h in range(HP):
                ins = mm(PS[:, 1024 + 256 * h:1024 + 256 * (h + 1)], LW[64:128, P * h:P * (h + 1)], L1[64:128, :])
            ins.then_inc(a_ps, 1)
            pe.wait_ge(win[2], 16)
            for i in range(4):
                tile(6 + i, lambda k: cols(3, 512)[:, k, P * i:P * (i + 1)])
            pe.wait_ge(masks, 5)
            pe.wait_ge(sq_ok, 1)
            pe.wait_ge(sz_ok, 4)
            for h in range(HP):
                ins = mm(PS[:, 256 * h:256 * (h + 1)], BD[:, :], hp3(BF)[:, h])
            ins.then_inc(ss_ps, 1)
            pe.wait_ge(win[3], 16)
            for i in range(4):
                tile(10 + i, lambda k: cols(5, 512)[:, k, P * i:P * (i + 1)])
            pe.wait_ge(win[4], 16)
            for i in range(4):
                tile(14 + i, lambda k: cols(7, 512)[:, k, P * i:P * (i + 1)])
            tile(18, lambda k: DGW[:, 16 * k:16 * (k + 1)])
            pe.wait_ge(win[5], 16)
            pe.wait_ge(iclr_ok, 4)
            for t in range(TT):
                for k in range(KC):
                    ins = mm(bank(2 + t), UT3[:, k, P * t:P * (t + 1)], cols(9, 512)[:, k, :], k == 0, k == KC - 1)
                ins.then_inc(gv_ps, 1)
                if t == 0:
                    pe.wait_ge(tile_g, 5)
                    for h in range(2):
                        ins = mm(bank(7)[:, 256 * h:256 * (h + 1)], GK2[0:16, P * h:P * (h + 1)], DGK[0:16, :])
                    ins.then_inc(gk_ps, 1)

            pe.wait_ge(tile_v, 14)
            pe.wait_ge(ss_max, 1)
            for grp in TOK_ORDER:
                t = grp % 2
                if grp == 4:
                    pe.wait_ge(exp_used, 2)
                if grp == 6:
                    pe.wait_ge(a_ok, 4)
                if grp == 7:
                    pe.wait_ge(gk_read, 2)
                if grp == 2:
                    pe.wait_ge(kf_ok, 1)
                    pe.wait_ge(gvg_ok, 2)
                for h in range(HP):
                    src = (hp3(T4)[:, h, P * t:P * (t + 1)], hp3(KF)[:, h, P * t:P * (t + 1)], hp3(BF)[:, h, P * t:P * (t + 1)],
                           AR5[:, h, t, 0, :])[grp // 2]
                    ins = pe.transpose(bank(grp)[:, P * h:P * (h + 1)], src, ID[:, :])
                ins.then_inc(tok_ps, 1)
            pe.wait_ge(win[6], 16)
            pe.wait_ge(win[7], 16)
            for t in range(TT):
                pe.wait_ge(tok_a, t + 1)
                for half, s in ((0, 11), (1, 0)):
                    for k in range(KC):
                        ins = mm(bank(t)[:, 256 * half:256 * (half + 1)], UT3[:, k, P * t:P * (t + 1)], cols(s, 256)[:, k, :],
                                 k == 0, k == KC - 1)
                ins.then_inc(gg_ps, 1)
            pe.wait_ge(rkk_ok, 1)
            pe.wait_ge(tok_v, 3)
            for t in range(TT):
                for h in range(HP):
                    ins = mm(bank(2)[:, 8 * t + 2 * h:8 * t + 2 * h + 2], hp3(T2)[:, h, P * t:P * (t + 1)], BD[:, 0:P:64])
            ins.then_inc(bon_ps, 1)

            pe.wait_ge(tok_a, 4)
            pe.wait_ge(tok_v, 4)
            pe.wait_ge(r_ok, 1)
            for u in range(8):
                t, h = u // 4, u % 4
                b0 = 4 * ((u + 1) % 2)
                if u == 1:
                    pe.wait_ge(bon_ok, 1)
                    pe.wait_ge(gvg_ok, 4)
                if u >= 2:
                    pe.wait_ge(mat_ok, u - 1)
                for j in range(2):
                    r = slice(64 * j, 64 * j + 64)
                    mm(bank(b0 + j)[:, 0:256], hp3(BF)[r, h, P * t:P * (t + 1)], AR5[r, h, t, :, :])
                for j in range(2):
                    r = slice(64 * j, 64 * j + 64)
                    mm(bank(b0 + j)[:, 256:512], hp3(KF)[r, h, P * t:P * (t + 1)], AR5[r, h, t, :, :])
                for j in range(2):
                    r = slice(64 * j, 64 * j + 64)
                    ins = mm(bank(b0 + 2 + j)[:, 0:P], AR5[r, h, t, 0, :], hp3(BF)[r, h, P * t:P * (t + 1)])
                ins.then_inc(mat_ps, 1)

            pe.wait_ge(mat_ok, 7)
            pe.wait_ge(gla_el, 1)
            for t in range(TT):
                for h in range(2):
                    ins = pe.transpose(bank(4)[:, 256 * t + P * h:256 * t + P * (h + 1)], KL[:, h, P * t:P * (t + 1)], ID[:, :])
            ins.then_inc(klt_ps, 1)
            for t in range(TT):
                for q in range(2):
                    for j in range(2):
                        r = slice(64 * j, 64 * j + 64)
                        ins = mm(bank(5 + j)[:, 256 * t + P * q:256 * t + P * (q + 1)], KE[r, q, P * t:P * (t + 1)], QE[r, q, P * t:P * (t + 1)])
            ins.then_inc(att_ps, 1)
            mm(bank(7), L2[:, 0:P], G2[:, :]).then_inc(gate_ps, 1)
            pe.wait_ge(klt_ok, 1)
            mm(bank(4), L2[:, P:2 * P], G2[:, :]).then_inc(gate_ps, 1)

            def gla_added(c):
                t, r = c // 2, slice(64 * (c % 2), 64 * (c % 2) + 64)
                for h in range(2):
                    ins = mm(bank(3)[:, 256 * h:256 * (h + 1)], KLT[r, t, h, :], GV[r, 512 * t + 256 * h:512 * t + 256 * (h + 1)])
                ins.then_inc(sg_ps, 1)

            def gla_state(c):
                t, r = c // 2, slice(64 * (c % 2), 64 * (c % 2) + 64)
                pe.wait_ge(sg_ok, c)
                for h in range(2):
                    ins = mm(bank(GO[t])[r, 256 * h:256 * (h + 1)], QB[:, h, L * c:L * (c + 1)], SG[:, 256 * h:256 * (h + 1)],
                             False, c == 3, True)
                ins.then_inc(go_used if c < 3 else go_ps, 1)

            def gla_intra():
                for t in range(TT):
                    for h in range(GH):
                        mm(bank(GO[t])[:, P * h:P * (h + 1)], ATT[:, t, h, :], GV[:, 512 * t + P * h:512 * t + P * (h + 1)], h == 0, False, True)

            pe.wait_ge(mat_ok, 8)
            pe.wait_ge(x1_ok, 8)
            pe.wait_ge(x1t_ok, 8)
            for lv in range(5):
                for g in range(4):
                    if lv == 0 and g == 2:
                        pe.wait_ge(att_ok, 2)
                        pe.wait_ge(gate_ok, 2)
                    if lv:
                        pe.wait_ge(xx_ok, 2 * (4 * (lv - 1) + g + 1))
                    for q in range(4):
                        ins = mm(bank(2 * g)[:, P * q:P * (q + 1)], MT[:, 4 * g + q, 0:P], X_[:, 4 * g + q, :])
                    ins.then_inc(y_ps, 1)
                if lv == 4:
                    gla_intra()
                    gla_added(0)
                for g in range(4):
                    if lv == 4 and g == 2:
                        gla_state(1)
                        gla_added(1)
                    pe.wait_ge(y_ok, 4 * lv + g + 1)
                    if lv < 4:
                        for q in range(4):
                            mm(bank(2 * g + 1)[:, P * q:P * (q + 1)], XT_[:, 4 * g + q, :], Y_[:, 4 * g + q, :])
                    for q in range(4):
                        ins = mm(bank(2 * g)[:, P * q:P * (q + 1)], Y_[:, 4 * g + q, :], XT_[:, 4 * g + q, :])
                    ins.then_inc(xx_ps, 1)
            for g in range(4):
                t = g // 2
                pe.wait_ge(xx_ok, 2 * 16 + g + 1)
                for q in range(4):
                    h = 4 * (g % 2) + q
                    ins = mm(bank(2 * g)[:, 64 * q:64 * (q + 1)], MT[:, 4 * g + q, 256:384], Vt[:, 512 * t + 64 * h:512 * t + 64 * (h + 1)])
                ins.then_inc(mv_ps, 1)
            gla_state(2)
            gla_added(2)
            for g in range(4):
                pe.wait_ge(mv_ok, g + 1)
                for q in range(4):
                    ins = mm(bank(2 * g)[:, P * q:P * (q + 1)], XT_[:, 4 * g + q, :], AY4[:, g // 2, 4 * (g % 2) + q, :])
                ins.then_inc(wu_ps, 1)
            pe.wait_ge(wu_ok, 2)
            hb = (2, 4, 3)
            gb = (6, 6)
            rb = (3, 2)
            stb = (4, 2)

            def added(c):
                t, r = c // 2, slice(64 * (c % 2), 64 * (c % 2) + 64)
                for h in range(HP):
                    o = bank(hb[c])[:, P * h:P * (h + 1)]
                    tok = slice(512 * t + P * h, 512 * t + P * (h + 1))
                    mm(o, Bt[r, tok], U0[r, t, P * h:P * (h + 1)], True, False)
                    ins = mm(o, Kt[r, tok], Vt[r, tok], False, True)
                ins.then_inc(h_ps, 1)

            def transition(c):
                t, r = c // 2, slice(64 * (c % 2), 64 * (c % 2) + 64)
                for h in range(HP):
                    ins = mm(bank(gb[c - 1])[:, P * h:P * (h + 1)], WM[r, t, P * h:P * (h + 1)], Bt[r, 512 * t + P * h:512 * t + P * (h + 1)])
                ins.then_inc(gt_ps, 1)

            def state(c):
                b = stb[c - 1]
                pe.wait_ge(st_ok, c)
                mm(bank(b), ID[:, :], SRW[:, c - 1].rearrange("p h w -> p (h w)"), True, False, True)
                for h in range(HP):
                    ins = mm(bank(b)[:, P * h:P * (h + 1)], GTS[:, c - 1, h, :], SRW[:, c - 1, h, :], False, h == HP - 1, True)
                ins.then_inc(st_ps, 1)

            def out_intra(t):
                for h in range(NH):
                    o = bank(t)[:, 64 * h:64 * (h + 1)]
                    mm(o, MT[:, 8 * t + h, P:2 * P], U0[:, t, 64 * h:64 * (h + 1)], h == 0, False, True)
                    mm(o, MT[:, 8 * t + h, 384:512], Vt[:, 512 * t + 64 * h:512 * t + 64 * (h + 1)], False, False, True)

            def out_state(c):
                t, r = c // 2, slice(64 * (c % 2), 64 * (c % 2) + 64)
                pe.wait_ge(st_ok, c)
                for h in range(HP):
                    ins = mm(bank(t)[r, P * h:P * (h + 1)], REFF[:, t, h, 64 * (c % 2):64 * (c % 2) + 64], SRW[:, c - 1, h, :],
                             False, c == 3, True)
                return ins

            added(0)
            out_intra(0)
            pe.wait_ge(wu_ok, 4)
            transition(1)
            added(1)
            gla_state(3)
            state(1)
            for t in range(TT):
                for h in range(NH):
                    r = slice(64 * (h % 2), 64 * (h % 2) + 64)
                    ins = mm(bank(rb[t])[r, P * (h // 2):P * (h // 2 + 1)], WM[:, t, 64 * h:64 * (h + 1)], MT[:, 8 * t + h, P:2 * P])
                ins.then_inc(reff_ps, 1)
            transition(2)
            out_intra(1)
            pe.wait_ge(reff_ok, 2)
            added(2)
            state(2)
            out_state(1)
            out_state(2)
            out_state(3).then_inc(o_ps, 1)

            pe.wait_ge(y_gla, 1)
            transposes(YT, range(4, 8))
            pe.wait_ge(wout_in, 16)
            wo = slot(4, 4).rearrange("p (k n) -> p k n", k=KC)

            def w_out_product(k, t, half):
                return mm(bank(4 + 2 * t + half), UT3[:, k, P * t:P * (t + 1)], wo[:, k, 512 * half:512 * (half + 1)],
                          k == 4, k == 3, True)

            for k in range(4, 8):
                pe.wait_ge(ut_a, k + 1)
                for t in range(TT):
                    for half in range(2):
                        w_out_product(k, t, half)
            pe.wait_ge(y_rw, 1)
            transposes(YT, range(4))
            pe.wait_ge(ut_a, 10)
            pe.wait_ge(ut_v, 6)
            for t in range(TT):
                for half in range(2):
                    for k in range(4):
                        ins = w_out_product(k, t, half)
                ins.then_inc(wout_used if t else wout_ps, 1)
            pe.wait_ge(scaled, 2)
            transposes(XB3)
            pe.wait_ge(ut_a, 14)
            pe.wait_ge(ut_v, 10)
            for t in range(TT):
                o = bank(6)[:, NE * t:NE * (t + 1)]
                for k in range(KC):
                    ins = mm(o, UT3[:, k, P * t:P * (t + 1)], WR3[:, k, :], k == 0, k == KC - 1)
            ins.then_inc(lg_ps, 1)
            def open_sums(t):
                for half in range(2):
                    ins = mm(bank(2 * t + half), OHGT[:, 0:P], XB3[:, t, 512 * half:512 * (half + 1)], True, False, True)
                ins.then_inc(zero_ps, 1)

            open_sums(0)
            pe.wait_ge(brow_in, 48)
            for i in range(16):
                ins = pe.transpose(bank(5)[:, NE * i:NE * (i + 1)], B1R[0:NE, P * i:P * (i + 1)], ID[0:NE, 0:NE])
            ins.then_inc(b1_ps, 1)
            pe.wait_ge(sel_ok, 1)
            ms = RT8[3]
            mm(bank(7)[:, 0:NE], SU[:, :], ms[:, 0, 0:NE])
            mm(bank(7)[:, NE:2 * NE], ONES[:, :], ms[:, 0, 0:NE], True, False)
            mm(bank(7)[:, NE:2 * NE], SU[:, :], ms[:, 1, 0:NE], False, True)
            mm(bank(7)[:, 2 * NE:3 * NE], ONES[:, :], ms[:, 0, 0:NE], True, False)
            mm(bank(7)[:, 2 * NE:3 * NE], ONES[:, :], ms[:, 1, 0:NE], False, True).then_inc(pos_ps, 1)
            open_sums(1)

            def gather():
                for k in range(KC):
                    for t in range(TT):
                        ins = mm(bank(6)[:, SLOTS * k:SLOTS * (k + 1)], XB3[:, t, P * k:P * (k + 1)], OH3[:, t, :],
                                 k == 0 and t == 0, t == 1, True)
                ins.then_inc(gathered, 1)

            def scatter(done, last=False):
                for t in range(TT):
                    for half in range(2):
                        r = slice(64 * half, 64 * half + 64)
                        ins = mm(bank(2 * t + half), OHGT[r, P * t:P * (t + 1)], YS[r, :], False, last, True)
                ins.then_inc(done, 1)

            pe.wait_ge(oh_ok, 1)
            gather()
            pe.wait_ge(gates_ok, 2)
            for t in range(TT):
                ins = pe.transpose(bank(7)[:, P * t:P * (t + 1)], OHG3[:, t, :], ID[:, :])
            ins.then_inc(gtt_ps, 1)
            pe.wait_ge(gt_ok, 1)
            pe.wait_ge(cnt_ok, 1)
            pe.wait_ge(b1_ok, 1)

            def item(i, h, odd):
                pe.wait_ge(xg_ok, i + 1)
                pe.wait_ge(t_ok, i * 2 + 1)
                if odd:
                    pe.wait_ge(landed_x[START], h * 16 + 32)
                else:
                    pe.wait_ge(landed[START], h * 16 + 16)
                for k in range(KC):
                    if k >= XSLOT:
                        pe.wait_ge(landed[k], h * 32 + 16 * (odd + 1))
                    elif odd:
                        pe.wait_ge(landed_x[k], h * 16 + 32)
                    else:
                        pe.wait_ge(landed[k], h * 16 + 16)
                    w = XTRA[k] if odd and k < XSLOT else slot(k)
                    for half in range(2):
                        mm(bank(4 + half)[0:64, :], XG[:, k, :], w[:, 512 * half:512 * (half + 1)], k == 0, k == KC - 1, True)
                        ins = mm(bank(4 + half)[64:128, :], XG[:, k, :], w[:, FF + 512 * half:FF + 512 * (half + 1)], k == 0, k == KC - 1, True)
                        if k == KC - 1 and half == 0:
                            ins.then_inc(h0_ps, 1)
                    ins.then_inc(w1_used, 1)
                pe.wait_ge(ys_ok, i + 1)
                scatter(scattered)
                pe.wait_ge(ohg_ok, i + 1)
                for t in range(TT):
                    ins = pe.transpose(bank(7)[:, P * t:P * (t + 1)], OHG3[:, t, :], ID[:, :])
                ins.then_inc(ohgt_ps, 1)
                pe.wait_ge(hs0, i + 1)
                for c in range(KC):
                    if c == 4:
                        pe.wait_ge(hs1, i + 1)
                    ins = pe.transpose(bank(4 + c // 4)[:, P * (c % 4):P * (c % 4 + 1)], HS[:, P * c:P * (c + 1)], ID[:, :])
                    if c % 4 == 3:
                        ins.then_inc(t_ps, 1)
                pe.wait_ge(oh_ok, i + 2)
                gather()
                pe.wait_ge(ohgt_ok, i + 1)
                for k in range(KC):
                    if k % 4 == 0:
                        pe.wait_ge(act_ok, i * 2 + (k // 4 + 1))
                    if k % 2 == 0:
                        pe.wait_ge(landed[8 + k // 2], h * 32 + 16 * (odd + 1))
                    w = slot(8 + k // 2)[:, 1024 * (k % 2):1024 * (k % 2 + 1)]
                    mm(bank(7)[0:64, :], ACTT[:, k, :], w[:, 0:512], k == 0, k == KC - 1, True)
                    ins = mm(bank(7)[64:128, :], ACTT[:, k, :], w[:, 512:1024], k == 0, k == KC - 1, True)
                    if k % 2:
                        ins.then_inc(w2_used, 1)

            def experts(nb):
                with pe.Fori(0, NE // 2) as h:
                    for odd in range(2):
                        for b in range(nb):
                            item(h * (2 * nb) + (odd * nb + b), h, odd)
                pe.wait_ge(ple_in, 32)
                for k in range(2):
                    for t in range(TT):
                        ins = pe.transpose(bank(4)[:, 256 * k + P * t:256 * k + P * (t + 1)], PX[:, t, P * k:P * (k + 1)], ID[:, :])
                ins.then_inc(pt_ps, 1)
                pe.wait_ge(ys_ok, NE * nb + 1)
                scatter(acc_done, True)

            most = pe.value_load(CNTI[0:1, 0:1], min_val=0, max_val=T)
            with pe.If(most > SLOTS):
                experts(NBMAX)
            with pe.Else():
                experts(1)

            pe.wait_ge(pt_ok, 1)
            for t in range(TT):
                for half in range(2):
                    for k in range(2):
                        ins = mm(bank(4 + 2 * t + half), PT[:, k, P * t:P * (t + 1)], PLW[:, k, 512 * half:512 * (half + 1)], k == 0, k == 1)
                if t == 0:
                    pe.wait_ge(scaled, 4)
                    transposes(XB3)
            ins.then_inc(pw_ps, 1)
            pe.wait_ge(wout_in, 32)
            pe.wait_ge(ut_a, 18)
            pe.wait_ge(ut_v, 14)
            for t in range(TT):
                for half in range(2):
                    for k in range(KC):
                        ins = mm(bank(2 * t + half), UT3[:, k, P * t:P * (t + 1)], PLG[:, k, 512 * half:512 * (half + 1)], k == 0, k == KC - 1)
                    ins.then_inc(pg_ps, 1)


_INS = ["x", "p", "norm_mix", "w_in", "shift_mu", "rw_w0", "rw_w2", "rw_a0", "rw_a2", "rw_g2", "rw_kk", "rw_ka", "rw_rk",
        "rw_gn_w", "rw_gn_b", "gla_gk2", "gla_gk_b", "gla_norm", "w_out", "norm_ffn", "w_router", "b_router",
        "w1", "b1", "w2", "b2", "norm_ple", "w_ple_gate", "w_ple", "norm_final"]


def kernel(**inputs):
    import numpy as _np
    import concourse.bacc as _bacc
    from concourse import mybir as _mybir
    from concourse.bass_utils import run_bass_kernel_spmd as _run

    nc = _bacc.Bacc("TRN2", target_bir_lowering=False, num_devices=1)
    arrays, args = {}, []
    for name in _INS:
        a = _np.ascontiguousarray(inputs[name])
        arrays[f"in_{name}_dram"] = a
        args.append(nc.dram_tensor(f"in_{name}_dram", a.shape, _mybir.dt.from_np(a.dtype), kind="ExternalInput").ap())
    args.append(nc.dram_tensor("out_0_dram", (1, T, D), F32, kind="ExternalOutput").ap())
    hybrid_block(nc, *args)
    r = _run(nc, [arrays], core_ids=[0])
    return r.results[0]["out_0_dram"]
```
